# Optimizing a Trainium2 kernel written in Bass

```python
import jax
import jax.numpy as jnp
from jax import lax
import numpy as np

D_MODEL = 2048
BATCH = 1
SEQ = 512
DEPTH = 1

GRID_W = 64
CTX_LEN = 256
NORM_EPS = 1e-6
N_ADA = 6
D_LRU = D_MODEL // 2
LRU_HEADS = D_LRU // 128
LRU_BW = D_LRU // LRU_HEADS
CONV_W = 4
CONV_LEFT = 2
RGLRU_C = 8.0
D_POOL = D_MODEL // 4
POOL_WINDOWS = (2, 4, 8, 16)
N_POOL_GROUPS = len(POOL_WINDOWS)
POOL_GC = D_POOL // N_POOL_GROUPS
POOL_OUT_GC = D_MODEL // N_POOL_GROUPS
D_FOURIER = D_MODEL // 4
FOURIER_GROUPS = 4
FOURIER_GC = D_FOURIER // FOURIER_GROUPS
N_BRANCHES = 3
I_YA = D_LRU
I_XB = 2 * D_LRU
I_XC = I_XB + D_POOL
I_G = I_XC + D_FOURIER
D_IN = I_G + N_BRANCHES * D_MODEL
D_FF = ((8 * D_MODEL + 3 * 256 - 1) // (3 * 256)) * 256

kernel_name = "hybrid_gated_lru_pool_fourier_dit"

def _rms_norm(x, g):
    xf = x.astype(jnp.float32)
    y = xf * lax.rsqrt(jnp.mean(xf * xf, axis=-1, keepdims=True) + NORM_EPS)
    return (y * g.astype(jnp.float32)).astype(x.dtype)

def _modulate(h, shift, scale):
    return h * (1 + scale) + shift

def _centred_depthwise_conv(x, w, b):
    y = lax.conv_general_dilated(
        x, w[:, None, :].astype(x.dtype), window_strides=(1,),
        padding=[(CONV_LEFT, CONV_W - 1 - CONV_LEFT)],
        dimension_numbers=('NWC', 'WIO', 'NWC'), feature_group_count=x.shape[-1])
    return y + b

def _lin_combine(left, right):
    a1, b1 = left
    a2, b2 = right
    return a1 * a2, a2 * b1 + b2

def _rglru_scan(xc, wa, ba, wx, bx, lam, h0, reverse):
    B, L, _ = xc.shape
    f32 = jnp.float32
    xf = xc.astype(f32)
    xh = xf.reshape(B, L, LRU_HEADS, LRU_BW)
    r = jax.nn.sigmoid(jnp.einsum('blhi,hij->blhj', xh, wa.astype(f32)) + ba.astype(f32)).reshape(B, L, D_LRU)
    i = jax.nn.sigmoid(jnp.einsum('blhi,hij->blhj', xh, wx.astype(f32)) + bx.astype(f32)).reshape(B, L, D_LRU)
    log_a = -RGLRU_C * r * jax.nn.softplus(-lam.astype(f32))
    a = jnp.exp(log_a)
    b = jnp.sqrt(-jnp.expm1(2.0 * log_a)) * (i * xf)
    a_cum, h = lax.associative_scan(_lin_combine, (a, b), axis=1, reverse=reverse)
    return h + a_cum * h0.astype(f32)[:, None, :]

def _bidir_rglru(xa, conv_w, conv_b, lru_wa, lru_ba, lru_wx, lru_bx, lru_lambda, h0_f, h0_b):
    xconv = _centred_depthwise_conv(xa, conv_w, conv_b)
    h_f = _rglru_scan(xconv, lru_wa[0], lru_ba[0], lru_wx[0], lru_bx[0], lru_lambda[0], h0_f, False)
    h_b = _rglru_scan(xconv, lru_wa[1], lru_ba[1], lru_wx[1], lru_bx[1], lru_lambda[1], h0_b, True)
    return h_f, h_b

def _multiscale_pool(xb, rows, w_pool, pool_scale):
    B, L, _ = xb.shape
    width = L // rows
    xg = xb.astype(jnp.float32).reshape(B, rows, width, N_POOL_GROUPS, POOL_GC)
    cs = jnp.pad(jnp.cumsum(xg, axis=2), ((0, 0), (0, 0), (1, 0), (0, 0), (0, 0)))
    t = jnp.arange(width)[:, None]
    win = jnp.array(POOL_WINDOWS, jnp.int32)[None, :]
    lo = jnp.clip(t - win // 2, 0, width)
    hi = jnp.clip(t - win // 2 + win, 0, width)
    grp = jnp.arange(N_POOL_GROUPS)[None, :]
    window_sum = cs[:, :, hi, grp] - cs[:, :, lo, grp]
    mean = window_sum / (hi - lo).astype(jnp.float32)[:, :, None]
    pooled = (mean - xg).reshape(B, L, N_POOL_GROUPS, POOL_GC).astype(xb.dtype)
    y = jnp.einsum('blgi,gio->blgo', pooled, w_pool).reshape(B, L, D_MODEL)
    return y * pool_scale

def _fourier_mix(xc, w_fourier):
    B, L, _ = xc.shape
    xg = xc.astype(jnp.float32).reshape(B, L, FOURIER_GROUPS, FOURIER_GC)
    f = jnp.fft.fft2(xg, axes=(1, 3), norm='ortho').real
    return f.reshape(B, L, D_FOURIER).astype(xc.dtype) @ w_fourier

def _mixer(u, rows, h0_f, h0_b, w_in, conv_w, conv_b, lru_wa, lru_ba, lru_wx, lru_bx, lru_lambda,
           w_lru_out, w_pool, pool_scale, w_fourier, b_gate, w_out):
    xa, ya, xb, xc, gl = jnp.split(u @ w_in, [I_YA, I_XB, I_XC, I_G], axis=-1)
    h_f, h_b = _bidir_rglru(xa, conv_w, conv_b, lru_wa, lru_ba, lru_wx, lru_bx, lru_lambda, h0_f, h0_b)
    lru_out = ((h_f + h_b).astype(u.dtype) * jax.nn.gelu(ya)) @ w_lru_out
    pool_out = _multiscale_pool(xb, rows, w_pool, pool_scale)
    four_out = _fourier_mix(xc, w_fourier)
    g_lru, g_pool, g_four = jnp.split(jax.nn.sigmoid(gl + b_gate), N_BRANCHES, axis=-1)
    merged = g_lru * lru_out + g_pool * pool_out + g_four * four_out
    return merged @ w_out, h_f, h_b

def _swiglu(u, w_ffn_in, w_ffn_out):
    gate, up = jnp.split(u @ w_ffn_in, 2, axis=-1)
    return (jax.nn.silu(gate) * up) @ w_ffn_out

def setup_inputs(seed: int = 0) -> dict:
    key = jax.random.key(seed)
    ks = jax.random.split(key, 26)
    f32 = jnp.float32

    def nrm(k, shape, scale):
        return jax.random.normal(k, shape, f32) * scale

    a_init = jax.random.uniform(ks[15], (DEPTH, 2, D_LRU), f32, 0.9, 0.999) ** (1.0 / RGLRU_C)
    return {
        'x': nrm(ks[0], (BATCH, SEQ, D_MODEL), 1.0),
        'c': nrm(ks[1], (BATCH, D_MODEL), 1.0),
        'ctx': nrm(ks[2], (BATCH, CTX_LEN, D_MODEL), 1.0),
        'c_ctx': nrm(ks[3], (D_MODEL,), 1.0),
        'w_ada': nrm(ks[4], (DEPTH, D_MODEL, N_ADA * D_MODEL), 0.5 * D_MODEL ** -0.5),
        'b_ada': nrm(ks[5], (DEPTH, N_ADA * D_MODEL), 0.1),
        'norm1_g': 1.0 + nrm(ks[6], (DEPTH, D_MODEL), 0.05),
        'norm2_g': 1.0 + nrm(ks[7], (DEPTH, D_MODEL), 0.05),
        'w_in': nrm(ks[8], (DEPTH, D_MODEL, D_IN), D_MODEL ** -0.5),
        'conv_w': nrm(ks[9], (DEPTH, CONV_W, D_LRU), CONV_W ** -0.5),
        'conv_b': nrm(ks[10], (DEPTH, D_LRU), 0.02),
        'lru_wa': nrm(ks[11], (DEPTH, 2, LRU_HEADS, LRU_BW, LRU_BW), LRU_BW ** -0.5),
        'lru_ba': nrm(ks[12], (DEPTH, 2, LRU_HEADS, LRU_BW), 0.02),
        'lru_wx': nrm(ks[13], (DEPTH, 2, LRU_HEADS, LRU_BW, LRU_BW), LRU_BW ** -0.5),
        'lru_bx': nrm(ks[14], (DEPTH, 2, LRU_HEADS, LRU_BW), 0.02),
        'lru_lambda': jnp.log(a_init) - jnp.log1p(-a_init),
        'w_lru_out': nrm(ks[16], (DEPTH, D_LRU, D_MODEL), D_LRU ** -0.5),
        'w_pool': nrm(ks[17], (DEPTH, N_POOL_GROUPS, POOL_GC, POOL_OUT_GC), POOL_GC ** -0.5),
        'pool_scale': 1.0 + nrm(ks[18], (DEPTH, D_MODEL), 0.05),
        'w_fourier': nrm(ks[19], (DEPTH, D_FOURIER, D_MODEL), D_FOURIER ** -0.5),
        'b_gate': nrm(ks[20], (DEPTH, N_BRANCHES * D_MODEL), 0.02),
        'w_out': nrm(ks[21], (DEPTH, D_MODEL, D_MODEL), D_MODEL ** -0.5),
        'w_ffn_in': nrm(ks[22], (DEPTH, D_MODEL, 2 * D_FF), D_MODEL ** -0.5),
        'w_ffn_out': nrm(ks[23], (DEPTH, D_FF, D_MODEL), D_FF ** -0.5),
        'norm_f_g': 1.0 + nrm(ks[24], (D_MODEL,), 0.05),
    }

def reference(x, c, ctx, c_ctx, w_ada, b_ada, norm1_g, norm2_g, w_in, conv_w, conv_b,
              lru_wa, lru_ba, lru_wx, lru_bx, lru_lambda, w_lru_out, w_pool, pool_scale,
              w_fourier, b_gate, w_out, w_ffn_in, w_ffn_out, norm_f_g):
    rows = x.shape[1] // GRID_W
    silu_c = jax.nn.silu(c)
    silu_cc = jax.nn.silu(c_ctx)
    h_zero = jnp.zeros((ctx.shape[0], D_LRU), jnp.float32)
    for l in range(DEPTH):
        last = l == DEPTH - 1
        mod = silu_c @ w_ada[l] + b_ada[l]
        mod_ctx = silu_cc @ w_ada[l] + b_ada[l]
        sh1, sc1, g1, sh2, sc2, g2 = jnp.split(mod[:, None, :], N_ADA, axis=-1)
        sh1c, sc1c, g1c, sh2c, sc2c, g2c = jnp.split(mod_ctx, N_ADA, axis=-1)
        lru_p = (conv_w[l], conv_b[l], lru_wa[l], lru_ba[l], lru_wx[l], lru_bx[l], lru_lambda[l])
        u_ctx = _modulate(_rms_norm(ctx, norm1_g[l]), sh1c, sc1c)
        if last:
            hc_f, hc_b = _bidir_rglru(u_ctx @ w_in[l][:, :D_LRU], *lru_p, h_zero, h_zero)
        else:
            mix_ctx, hc_f, hc_b = _mixer(u_ctx, 1, h_zero, h_zero, w_in[l], *lru_p, w_lru_out[l],
                                         w_pool[l], pool_scale[l], w_fourier[l], b_gate[l], w_out[l])
        h0_f = hc_f[:, -1]
        h0_b = hc_b[:, 0]
        u = _modulate(_rms_norm(x, norm1_g[l]), sh1, sc1)
        mix, _, _ = _mixer(u, rows, h0_f, h0_b, w_in[l], *lru_p, w_lru_out[l],
                           w_pool[l], pool_scale[l], w_fourier[l], b_gate[l], w_out[l])
        x = x + g1 * mix
        x = x + g2 * _swiglu(_modulate(_rms_norm(x, norm2_g[l]), sh2, sc2), w_ffn_in[l], w_ffn_out[l])
        if not last:
            ctx = ctx + g1c * mix_ctx
            ctx = ctx + g2c * _swiglu(_modulate(_rms_norm(ctx, norm2_g[l]), sh2c, sc2c),
                                      w_ffn_in[l], w_ffn_out[l])
    return _rms_norm(x, norm_f_g)


_drawn_inputs = setup_inputs


def setup_inputs(seed=0):
    import zlib

    import numpy as np

    out = dict(_drawn_inputs(seed))
    spreads = {}
    factors = {'norm2_g': 3.702, 'lru_ba': 55.615, 'lru_bx': 29.275, 'pool_scale': 7.342, 'b_gate': 8.0}
    for name, (base, spread) in spreads.items():
        noise = np.random.default_rng([zlib.crc32(name.encode()), seed]).standard_normal(out[name].shape)
        drawn = base * np.exp(spread * noise) if base else spread * noise
        out[name] = jnp.asarray(drawn.astype(out[name].dtype))
    for name, factor in factors.items():
        out[name] = (out[name] * factor).astype(out[name].dtype)
    return out
```

```python
from contextlib import ExitStack

import numpy as np

import concourse.bass as bass
from concourse import mybir

F32 = mybir.dt.float32
F32R = mybir.dt.float32r
ALU = mybir.AluOpType
ACT = mybir.ActivationFunctionType
ds = bass.ds

P = 128
D = 2048
T = 512
TC = 256
KT = D // P
GRID_W = 64
ROWS = T // GRID_W
D_LRU = D // 2
HEADS = D_LRU // P
I_YA, I_XB, I_G = D_LRU, 2 * D_LRU, 2 * D_LRU + D // 2
D_FF = ((8 * D + 3 * 256 - 1) // (3 * 256)) * 256
EPS = 1e-6
RGLRU_C = 8.0
TCAT = TC + T
PADX = TC + 5

RING = 4
UC = 4
UN = 256

NBLK = D_FF // (4 * P)
G_XA = 0
G_YX = G_XA + 16
G_MIX = G_YX + 32
G_OUT = G_MIX + 128
G_FF0 = G_OUT + 32
G_FF = G_FF0 + 16
G_FIN = G_FF + 24 * (NBLK - 1)
G_END = G_FIN + 8
POOL_AT = 4

Q_YX = 4
Q_FOUR = Q_YX + 8
Q_MIX = Q_FOUR + 4
Q_OUT = Q_MIX + 48
Q_FF0 = Q_OUT + 8
Q_FF = Q_FF0 + 4
Q_FIN = Q_FF + 12 * (NBLK - 1)

C_BADA, C_N1, C_N2 = 0, 96, 112
C_BG, C_PS, C_CW, C_CB, C_NF = 128, 176, 192, 224, 232
C_BA, C_BX, C_LAM, C_C, C_CC = 248, 264, 280, 296, 312
NPRM = 328
PRM_ROWS = (128, 120, 80)


class Chain:

    def __init__(self, eng, sem):
        self.eng, self.sem, self.n, self.shift = eng, sem, 0, 0

    def link(self, ins):
        self.n += 1
        ins.then_inc(self.sem, 1)
        self.eng.wait_ge(self.sem, self.n + self.shift)

    def enter(self, i, start, per):
        self.at, self.per = self.n, per
        self.shift = (i - start) * per

    def leave(self, times):
        assert self.n - self.at == self.per, (self.n - self.at, self.per)
        self.n, self.shift = self.at + self.per * times, 0


def build(nc, x, c, ctx_in, c_ctx, w_ada, b_ada, norm1_g, norm2_g, w_in, conv_w, conv_b, lru_wa, lru_ba,
          lru_wx, lru_bx, lru_lambda, w_lru_out, w_pool, pool_scale, w_fourier, b_gate, w_out,
          w_ffn_in, w_ffn_out, norm_f_g, consts, dft, out, x_fm):
    with ExitStack() as stack:
        kb = 1024
        at = 1152
        where = {}
        for region, size in (("raw", 16 * kb), ("hi", 16 * kb), ("u_hi", 32 * kb), ("u_lo", 32 * kb),
                             ("mix", 32 * kb), ("lru", 32 * kb), ("yx", 32 * kb), ("pf", 8 * kb),
                             ("gate", 4 * kb), ("ada", 12 * kb), ("misc", 5952)):
            where[region] = at
            at += size
        assert at <= nc.sbuf_usable_end, (at, nc.sbuf_usable_end)
        misc_at = [where["misc"]]

        def sb(name, region, shape, dt=F32, off=0):
            return nc.alloc_sbuf_tensor_at(name, [P, *shape], dt, offset=where[region] + off)

        def misc(name, shape):
            t = nc.alloc_sbuf_tensor_at(name, [P, *shape], F32, offset=misc_at[0])
            misc_at[0] += (4 * int(np.prod(shape)) + 31) // 32 * 32
            assert misc_at[0] <= where["misc"] + 5952, misc_at[0] - where["misc"]
            return t

        w_raw = sb("w_raw", "raw", [RING, UC, UN])
        w_lo = sb("w_lo", "raw", [RING, UC, UN], F32R)
        w_hi = sb("w_hi", "hi", [RING, UC, UN], F32R)
        u_hi = sb("u_hi", "u_hi", [KT, T], F32R)
        u_f = sb("u_f", "u_lo", [KT, T])
        u_lo = sb("u_lo", "u_lo", [KT, T], F32R)
        out_tm = sb("out_tm", "u_hi", [4, D])
        ctx_hi = sb("ctx_hi", "mix", [KT, TC], F32R)
        ctx_f = sb("ctx_f", "mix", [KT, TC], F32, 16 * kb)
        ctx_lo = sb("ctx_lo", "mix", [KT, TC], F32R, 16 * kb)
        x_stage = sb("x_stage", "mix", [2, KT, P])
        prm_rows = sb("prm_rows", "mix", [3, P], F32, 16 * kb)
        xcv = sb("xcv", "mix", [TCAT])
        la = sb("la", "mix", [2, TCAT], F32, 3 * kb)
        lb = sb("lb", "mix", [2, TCAT], F32, 9 * kb)
        lt = sb("lt", "mix", [2, TCAT], F32, 15 * kb)
        ld = sb("ld", "mix", [TCAT], F32, 21 * kb)
        lcs = sb("lcs", "mix", [TC], F32, 24 * kb)
        lh = sb("lh", "mix", [2, T], F32, 25 * kb)
        pw_a = sb("pw_a", "mix", [ROWS, 80])
        pw_b = sb("pw_b", "mix", [ROWS, 80], F32, 3 * kb)
        mixed = sb("mixed", "mix", [KT, T])
        ada_pc = sb("ada_pc", "lru", [4, 4, 512])
        pad = sb("pad", "lru", [HEADS, 1024])
        act_f = sb("act_f", "lru", [HEADS, 2, T])
        act_r = sb("act_r", "lru", [HEADS, 2, T], F32R)
        ff_f = sb("ff_f", "lru", [2, 2, 4, T])
        ff_r = sb("ff_r", "lru", [2, 2, 4, T], F32R)
        yx = sb("yx", "yx", [KT, T])
        four_lo = sb("four_lo", "yx", [4, T], F32R, 24 * kb)
        four_hi = sb("four_hi", "pf", [4, T], F32R)
        x_tok = sb("x_tok", "yx", [2, D])
        x_nrm = sb("x_nrm", "yx", [2, D], F32, 16 * kb)
        xcs = sb("xcs", "pf", [2, 4, 256])
        sq = sb("sq", "pf", [2, T])
        sq_acc = sb("sq_acc", "pf", [2, T], F32, 4 * kb)
        rstd_b = sb("rstd_b", "pf", [T])
        gate = sb("gate", "gate", [2, T])
        gate_w = sb("gate_w", "gate", [2, 2, 2, P])
        dft_t = sb("dft_t", "ada", [3, 2 * T])
        ada2_pc = sb("ada2_pc", "ada", [2, 1024])
        ada2_acc = sb("ada2_acc", "ada", [1024], F32, 8 * kb)
        x_res = sb("x_res", "ada", [2, 2, T])
        x_fin = sb("x_fin", "ada", [2, 2, T])

        const = misc("const", [640])
        ident, cs128, inv_cnt = const[:, 0:128], const[:, 128:384], const[:, 384:640]
        ones = misc("ones", [P])
        prm = misc("prm", [NPRM])
        cvec = misc("cvec", [KT, 2])
        mod1 = misc("mod1", [2, 2, KT])
        gsc1 = misc("gsc1", [2, KT])
        mod2 = misc("mod2", [64])
        gsc2 = misc("gsc2", [KT])
        c2 = misc("c2", [16])
        lam = misc("lam", [6, 16])
        ssum = misc("ssum", [6])
        rstd = misc("rstd", [6])
        rfin = misc("rfin", [4])
        eps_t = misc("eps_t", [1])

        main = stack.enter_context(nc.psum_tensor("main", [P, 4, 512], F32))
        aux = stack.enter_context(nc.psum_tensor("aux", [P, 4, 512], F32))
        aux_flat = aux[:, :, :].rearrange("p b n -> p (b n)")

        def sem(name):
            return stack.enter_context(nc.semaphore(name))

        unit_landed = [sem(f"unit_landed{s}") for s in range(RING)]
        const_landed = sem("const_landed")
        prm_landed = [sem(f"prm_landed{r}") for r in range(3)]
        tok_landed = [sem(f"tok_landed{s}") for s in range(2)]
        ada_landed = [sem(f"ada_landed{s}") for s in range(4)]
        gw_landed = [sem(f"gw_landed{s}") for s in range(2)]
        dft_landed = [sem(f"dft_landed{s}") for s in range(3)]
        ada2_landed = [sem(f"ada2_landed{s}") for s in range(2)]
        res_landed = [sem(f"res_landed{s}") for s in range(2)]
        x_stored = [sem(f"x_stored{s}") for s in range(2)]
        out_stored = sem("out_stored")
        hi_done, lo_done, unit_used = sem("hi_done"), sem("lo_done"), sem("unit_used")
        pair_free = [sem("pair_free0"), sem("pair_free1")]
        ctx_free = [sem("ctx_free0"), sem("ctx_free1")]
        act_chain, dve_chain = sem("act_chain"), sem("dve_chain")
        ones_set, prm_turned, prm_ready = sem("ones_set"), sem("prm_turned"), sem("prm_ready")
        cvec_ready = sem("cvec_ready")
        root_done, nrm_done = sem("root_done"), sem("nrm_done")
        raw_turned, raw_out = sem("raw_turned"), sem("raw_out")
        nrm_turned, nrm_out = sem("nrm_turned"), sem("nrm_out")
        ada_used, mod_out = sem("ada_used"), sem("mod_out")
        u_aff, u_hi_done, u_lo_done = sem("u_aff"), sem("u_hi_done"), sem("u_lo_done")
        nabs_ready, z_ready, c2_ready = sem("nabs_ready"), sem("z_ready"), sem("c2_ready")
        conv_done, gates_done, decay_done = sem("conv_done"), sem("gates_done"), sem("decay_done")
        tanh_done = sem("tanh_done")
        q_done, root_q, lru_done = sem("q_done"), sem("root_q"), sem("lru_done")
        gelu_done, prod_done, act_hi, act_lo = sem("gelu_done"), sem("prod_done"), sem("act_hi"), sem("act_lo")
        chunk_ready = sem("chunk_ready")
        chunk_used, four_hi_done, four_lo_done = sem("chunk_used"), sem("four_hi_done"), sem("four_lo_done")
        pool_done = sem("pool_done")
        gate_used = sem("gate_used")
        ada2_used = [sem("ada2_used0"), sem("ada2_used1")]
        acc_used = sem("acc_used")
        m_hi, m_lo = sem("m_hi"), sem("m_lo")
        sq_done, sq_added, ms_ready = sem("sq_done"), sem("sq_added"), sem("ms_ready")
        rms_ready, v_aff, v_hi, v_lo = sem("rms_ready"), sem("v_aff"), sem("v_hi"), sem("v_lo")
        hid_hi, hid_lo = sem("hid_hi"), sem("hid_lo")
        sq2_done, sq2_added = sem("sq2_done"), sem("sq2_added")
        fin_ready, fin_turned = sem("fin_ready"), sem("fin_turned")
        fin_out_a, fin_out_v = sem("fin_out_a"), sem("fin_out_v")
        sqf2_ready, ms2_ready, rms2_ready, rfin_ready = sem("sqf2_ready"), sem("ms2_ready"), sem("rms2_ready"), sem("rfin_ready")
        rows_scaled = [sem("rows_scaled_v"), sem("rows_scaled_a")]

        def landed(eng, base, per, i, u):
            eng.wait_ge(unit_landed[u % RING], (base // RING + u // RING + 1) * 16 + i * (16 * per // RING))

        def splits(base, per, i, u):
            if base < G_MIX:
                return base + u + 1 + i * per
            if base == G_MIX:
                return base + u + 1 - (u > POOL_AT) + i * (per - 1)
            return base + u + 1 - 8 + i * per

        in_t = w_in[0].rearrange("(c p) n -> p c n", p=P)
        ada_t = w_ada[0].rearrange("(c p) n -> p c n", p=P)
        lru_t = w_lru_out[0].rearrange("(c p) (g n) -> p c g n", p=P, n=2 * UN)
        four_t = w_fourier[0].rearrange("(c p) (g n) -> p c g n", p=P, n=2 * UN)
        pool_t = w_pool[0].rearrange("g p n -> p g n")
        out_t = w_out[0].rearrange("(c p) n -> p c n", p=P)
        ffi_t = w_ffn_in[0].rearrange("(c p) n -> p c n", p=P)
        ffo_t = w_ffn_out[0].rearrange("(c p) n -> p c n", p=P)

        block = stack.enter_context(nc.Block())

        @block.sync
        def _(sp):
            def unit(base, per, i, u, src, raw_only=False):
                if not (base == 0 and u < RING and isinstance(i, int) and i == 0):
                    sp.wait_ge(unit_used, base + u - RING + 1 + i * per)
                dst = w_raw[:, u % RING, 0, :] if raw_only else w_raw[:, u % RING, :, :]
                sp.dma_start(dst, src).then_inc(unit_landed[u % RING], 16)

            def ada_piece(col, j, used):
                if used is not None:
                    sp.wait_ge(ada_used, used)
                sp.dma_start(ada_pc[:, j, :, :], ada_t[:, 4 * j:4 * j + 4, col]).then_inc(ada_landed[j], 16)

            sp.dma_start(const[:, :], consts).then_inc(const_landed, 16)
            rows = [(0, 0, b_ada[0], 96), (0, 96, norm1_g[0], 16), (0, 112, norm2_g[0], 16),
                    (1, 0, b_gate[0], 48), (1, 48, pool_scale[0], 16), (1, 64, conv_w[0], 32),
                    (1, 96, conv_b[0], 8), (1, 104, norm_f_g, 16),
                    (2, 0, lru_ba[0], 16), (2, 16, lru_bx[0], 16), (2, 32, lru_lambda[0], 16),
                    (2, 48, c, 16), (2, 64, c_ctx, 16)]
            for r, first, src, n in rows:
                if len(src.shape) == 1:
                    src = src.rearrange("(a b) -> a b", b=P)
                elif len(src.shape) == 3:
                    src = src.rearrange("d h b -> (d h) b")
                else:
                    src = src.rearrange("d (a b) -> (d a) b", b=P)
                sp.dma_start(prm_rows[first:first + n, r, :], src).then_inc(prm_landed[r], 16)
            toks = [x[0, P * i:P * i + P, :] for i in range(4)] + [ctx_in[0, P * i:P * i + P, :] for i in range(2)]
            for i in range(2):
                sp.dma_start(x_tok[:, i, :], toks[i]).then_inc(tok_landed[i], 16)
            for j in range(4):
                ada_piece(slice(0, 512), j, None)
            for i in range(6):
                if i < 4:
                    sp.wait_ge(raw_out, 4 * (i + 1))
                    sp.dma_start(x_fm[:, :, P * i:P * i + P], x_stage[:, i % 2, :, :]).then_inc(x_stored[i % 2], 16)
                if i + 2 < 6:
                    sp.wait_ge(nrm_done, i + 1)
                    sp.wait_ge(raw_turned, 4 * min(i + 1, 4))
                    sp.dma_start(x_tok[:, i % 2, :], toks[i + 2]).then_inc(tok_landed[i % 2], 16)
            for u in range(RING):
                unit(0, 8, 0, u, in_t[:, UC * u:UC * u + UC, 0:UN])
            with sp.Fori(0, 3) as q:
                for j in range(4):
                    ada_piece(ds(D + 512 * q, 512), j, q * 8 + j + 1)
                for j in range(4):
                    ada_piece(ds(512 * q + 512, 512), j, q * 8 + j + 5)
            for j in range(4):
                ada_piece(slice(D + 1536, D + 2048), j, 24 + j + 1)
            with sp.Fori(1, 4) as i:
                for u in range(4):
                    unit(G_XA, 4, i, u, in_t[:, UC * u:UC * u + UC, ds(i * UN, UN)])

            def window(h, hh, p, base, per, i, u0):
                if not isinstance(h, int) or h >= 2:
                    sp.wait_ge(gates_done, h * 2 - 2)
                sp.dma_start(gate_w[:, p, 0, :, :], lru_wa[0][:, ds(h, 1), :, :].rearrange("d h i j -> (h i) d j")).then_inc(gw_landed[p], 16)
                sp.dma_start(gate_w[:, p, 1, :, :], lru_wx[0][:, ds(h, 1), :, :].rearrange("d h i j -> (h i) d j")).then_inc(gw_landed[p], 16)
                for u in range(4):
                    unit(base, per, i, u0 + u, in_t[:, UC * u:UC * u + UC, ds(h * UN + I_YA, UN)])

            window(0, 0, 0, G_YX, 4, 0, 0)
            with sp.Fori(0, 3) as i:
                window(i * 2 + 1, i, 1, G_YX + 4, 8, i, 0)
                window(i * 2 + 2, i + 1, 0, G_YX + 4, 8, i, 4)
            window(7, 3, 1, G_YX + 28, 4, 0, 0)
            for t in range(3):
                sp.dma_start(dft_t[:, t, :], dft[t]).then_inc(dft_landed[t], 16)

            with sp.Fori(0, 8) as i:
                def gcols(branch):
                    return ds(i * UN + (I_G + branch * D), UN)
                u = 0
                for what in ("pool", "four", "lru"):
                    for k in range(4):
                        unit(G_MIX, 16, i, u, in_t[:, UC * k:UC * k + UC, gcols(("lru", "pool", "four").index(what))])
                        u += 1
                    if what == "pool":
                        unit(G_MIX, 16, i, u, pool_t[:, ds(i // 2, 1), ds((i % 2) * UN, UN)].rearrange("p g n -> p (g n)"), raw_only=True)
                        u += 1
                    elif what == "four":
                        src = four_t[:, :, ds(i // 2, 1), ds((i % 2) * UN, UN)]
                        unit(G_MIX, 16, i, u, src.rearrange("p c g n -> p c (g n)"))
                        u += 1
                    else:
                        for k in range(2):
                            src = lru_t[:, UC * k:UC * k + UC, ds(i // 2, 1), ds((i % 2) * UN, UN)]
                            unit(G_MIX, 16, i, u, src.rearrange("p c g n -> p c (g n)"))
                            u += 1

            with sp.Fori(0, 4) as i:
                for j in range(2):
                    for k in range(4):
                        unit(G_OUT, 8, i, 4 * j + k, out_t[:, UC * k:UC * k + UC, ds((i * 2 + j) * UN, UN)])
                        if k == 1:
                            sp.wait_ge(ada2_used[j], 64)
                            sp.wait_ge(x_stored[0], 32)
                            sp.wait_ge(x_stored[1], 32)
                            sp.wait_ge(pair_free[j], i + Q_OUT // 2)
                            sp.dma_start(x_res[:, j, :, :], x_fm[:, ds(i * 4 + 2 * j, 2), :]).then_inc(res_landed[j], 16)

            def up(base, per, i, b):
                for g in range(4):
                    col = (g % 2) * D_FF + (g // 2) * UN
                    for k in range(4):
                        src = ffi_t[:, UC * k:UC * k + UC, ds(b * (2 * UN) + col, UN)]
                        unit(base, per, i, 4 * g + k, src)

            up(G_FF0, 16, 0, 0)
            with sp.Fori(0, NBLK - 1) as i:
                up(G_FF, 24, i, i + 1)
                for j in range(8):
                    unit(G_FF, 24, i, 16 + j, ffo_t[:, ds(i * UC, UC), UN * j:UN * j + UN])
            for j in range(8):
                unit(G_FIN, 8, 0, j, ffo_t[:, UC * (NBLK - 1):UC * NBLK, UN * j:UN * j + UN])
            for t in range(4):
                sp.wait_ge(rows_scaled[t % 2], t // 2 + 1)
                sp.dma_start(out[0, P * t:P * t + P, :], out_tm[:, t, :]).then_inc(out_stored, 16)
            sp.wait_ge(out_stored, 64)

        @block.scalar
        def _(act):
            chain = Chain(act, act_chain)

            def hi(base, per, i, u):
                landed(act, base, per, i, u)
                act.activation(w_hi[:, u % RING], w_raw[:, u % RING], ACT.Copy).then_inc(hi_done, 1)

            act.wait_ge(prm_ready, 1)
            act.activation(cvec[:, :, 0], prm[:, C_C:C_C + 16], ACT.Silu)
            act.activation(cvec[:, :, 1], prm[:, C_CC:C_CC + 16], ACT.Silu).then_inc(cvec_ready, 1)
            act.wait_ge(nabs_ready, 1)
            act.activation(lam[:, 2, :], lam[:, 1, :], ACT.Exp).then_inc(z_ready, 1)
            for i in range(6):
                act.wait_ge(tok_landed[i % 2], 16 * (i // 2 + 1))
                if i >= 2:
                    act.wait_ge(nrm_turned, 4 * (i - 1))
                chain.link(act.activation(x_nrm[:, i % 2, :], x_tok[:, i % 2, :], ACT.Square, accum_out=ssum[:, i:i + 1]))
                act.activation(rstd[:, i:i + 1], ssum[:, i:i + 1], ACT.Sqrt, bias=eps_t[:, :], scale=1.0 / D).then_inc(root_done, 1)
                if i < 4:
                    if i >= 2:
                        act.wait_ge(x_stored[i % 2], 16)
                    for q in range(4):
                        act.wait_ge(raw_turned, 4 * i + q + 1)
                        act.activation(x_stage[:, i % 2, 4 * q:4 * q + 4, :],
                                       main[:, q, :].rearrange("p (a b) -> p a b", b=P), ACT.Copy).then_inc(raw_out, 1)
            for u in range(2):
                hi(0, 8, 0, u)
            for s in range(2):
                act.wait_ge(x_stored[s], 32)
            with act.Fori(0, 4) as q:
                for t in range(4):
                    act.wait_ge(u_aff, q * 8 + 2 * t + 1)
                    act.activation(u_hi[:, ds(q * 4 + t, 1), :], u_f[:, ds(q * 4 + t, 1), :], ACT.Copy).then_inc(u_hi_done, 1)
                    act.wait_ge(u_aff, q * 8 + 2 * t + 2)
                    act.activation(ctx_hi[:, ds(q * 4 + t, 1), :], ctx_f[:, ds(q * 4 + t, 1), :], ACT.Copy).then_inc(u_hi_done, 1)

            with act.Fori(0, 2) as i:
                for u in range(8):
                    hi(G_XA, 8, i, u + 2)
                    if u % 4 == 3:
                        j = u // 4
                        if u == 3:
                            act.wait_ge(ada_used, 32)
                        act.wait_ge(unit_used, i * 8 + u + 1)
                        act.activation(pad[:, ds(i * 4 + 2 * j, 2), PADX:PADX + T], main[:, 2 * j:2 * j + 2, :],
                                       ACT.Copy).then_inc(pair_free[j], 1)

            def decay(h, d):
                hd = d * 8 + h
                act.wait_ge(gates_done, h * 2 + d + 1)
                act.activation(la[:, d, :], aux_flat[:, 256:1024], ACT.Tanh, bias=prm_h(C_BA, d, h), scale=0.5)
                act.activation(lb[:, d, :], aux_flat[:, 1280:2048], ACT.Tanh, bias=prm_h(C_BX, d, h), scale=0.5).then_inc(tanh_done, 1)
                act.wait_ge(tanh_done, h * 2 + d + 1)
                cc = c2[:, ds(hd, 1)]
                act.activation(lt[:, d, :], la[:, d, :], ACT.Tanh, bias=cc, scale=cc)
                act.activation(la[:, d, :], la[:, d, :], ACT.Exp, bias=cc, scale=cc).then_inc(decay_done, 1)

            def prm_h(col, d, h):
                return prm[:, ds(h + (col + 8 * d), 1)]

            def roots(h):
                for d in range(2):
                    act.wait_ge(q_done, h * 2 + d + 1)
                    act.activation(lt[:, d, :], lt[:, d, :], ACT.Sqrt).then_inc(root_q, 1)

            def window(h, p, base, per, i, u0, first=False):
                for u in range(4):
                    hi(base, per, i, u0 + u + 2)
                    if u == 0 and not first:
                        roots(h - 1)
                    if u == 2:
                        if not first:
                            act.wait_ge(lru_done, h)
                        decay(h, 0)
                    if u == 3:
                        decay(h, 1)
                act.wait_ge(unit_used, base + u0 + 4 + i * per)
                act.activation(yx[:, ds(h * 2, 2), :], main[:, 2 * p:2 * p + 2, :], ACT.Copy).then_inc(pair_free[p], 1)

            act.wait_ge(c2_ready, 1)
            window(0, 0, G_YX, 4, 0, 0, first=True)
            with act.Fori(0, 3) as i:
                window(i * 2 + 1, 1, G_YX + 4, 8, i, 0)
                window(i * 2 + 2, 0, G_YX + 4, 8, i, 4)
            window(7, 1, G_YX + 28, 4, 0, 0)

            def chunk_out(t):
                p = (Q_FOUR + t) % 2
                if t >= 2:
                    act.wait_ge(chunk_used, t - 1)
                if t == 2:
                    act.dma_start(dft_t[:, 0, :], dft[3]).then_inc(dft_landed[0], 16)
                act.wait_ge(chunk_ready, t + 1)
                act.activation(xcs[:, t % 2, :, :], main[:, 2 * p:2 * p + 2, :].rearrange("p b (g n) -> p (b g) n", n=256),
                               ACT.Copy).then_inc(pair_free[p], 1)

            chunk_out(0)
            chunk_out(1)
            roots(7)
            chunk_out(2)
            chunk_out(3)
            for p in range(2):
                act.wait_ge(pair_free[p], 6)
            for h in range(HEADS):
                act.activation(yx[:, h, :], yx[:, h, :], ACT.Gelu_apprx_tanh).then_inc(gelu_done, 1)
            act.wait_ge(chunk_used, 4)
            for g in range(4):
                act.activation(four_hi[:, g, :], aux[:, g, :], ACT.Copy).then_inc(four_hi_done, 1)
            for h in range(HEADS):
                act.wait_ge(prod_done, h + 1)
                act.activation(act_r[:, h, 0, :], act_f[:, h, 1, :], ACT.Copy).then_inc(act_hi, 1)

            with act.Fori(0, 8) as i:
                def ada2(cc):
                    s = cc % 2
                    act.wait_ge(ada2_used[s], i * 8 + cc // 2)
                    act.dma_start(ada2_pc[:, s, :], ada_t[:, cc, ds(i * 1024 + 2 * D, 1024)]).then_inc(ada2_landed[s], 16)

                for u in range(16):
                    if u + 2 != POOL_AT:
                        hi(G_MIX, 16, i, u + 2)
                    if u == 0:
                        ada2(0)
                    if u < 15:
                        ada2(u + 1)
                    if u in (3, 8, 13):
                        k = (3, 8, 13).index(u)
                        branch = (1, 2, 0)[k]
                        act.wait_ge(unit_used, i * 16 + (G_MIX + u + 1))
                        if k == 1:
                            act.wait_ge(pair_free[1], i * 3 + (Q_MIX // 2 + 1))
                        else:
                            act.wait_ge(gate_used, i * 2 + k // 2)
                        for n in range(2):
                            ins = act.activation(gate[:, n, :], main[:, n, :], ACT.Sigmoid,
                                                 bias=prm[:, ds(i * 2 + (C_BG + 16 * branch + n), 1)])
                        ins.then_inc(pair_free[0], 1)
            for k in range(KT):
                if k == 0:
                    act.wait_ge(gate_used, 16)
                act.activation(u_hi[:, k, :], mixed[:, k, :], ACT.Copy).then_inc(m_hi, 1)

            with act.Fori(0, 4) as i:
                for u in range(8):
                    hi(G_OUT, 8, i, u + 2)
                    if u % 4 == 3:
                        j = u // 4
                        act.wait_ge(pair_free[j], i + (Q_OUT // 2 + 1))
                        act.wait_ge(sq_added, i * 2 + j)
                        act.activation(sq[:, :, :], mixed[:, ds(i * 4 + 2 * j, 2), :], ACT.Square).then_inc(sq_done, 1)
            act.wait_ge(ms_ready, 1)
            act.activation(rstd_b[:, :], aux[:, 0, :], ACT.Sqrt, bias=eps_t[:, :], scale=1.0 / D).then_inc(rms_ready, 1)
            with act.Fori(0, 4) as q:
                for t in range(4):
                    act.wait_ge(v_aff, q * 4 + t + 1)
                    act.activation(u_hi[:, ds(q * 4 + t, 1), :], u_f[:, ds(q * 4 + t, 1), :], ACT.Copy).then_inc(v_hi, 1)

            def up_steps(base, per, i, b, q0, qi):
                pos = ds(b % 2, 1) if not isinstance(b, int) else slice(b % 2, b % 2 + 1)
                for u in range(16):
                    hi(base, per, i, u + 2)
                    pr = u // 8
                    if u % 8 == 3:
                        act.wait_ge(unit_used, base + u + 1 + i * per)
                        act.wait_ge(pair_free[1], q0 // 2 + pr + i * qi)
                        act.activation(gate[:, :, :], main[:, 0:2, :], ACT.Silu).then_inc(pair_free[0], 1)
                    if u % 8 == 7:
                        act.wait_ge(pair_free[1], q0 // 2 + pr + 1 + i * qi)
                        f = ff_f[:, pos, 1, 2 * pr:2 * pr + 2, :].rearrange("p o a n -> p (o a) n")
                        h = ff_r[:, pos, 0, 2 * pr:2 * pr + 2, :].rearrange("p o a n -> p (o a) n")
                        act.activation(h, f, ACT.Copy).then_inc(hid_hi, 1)

            up_steps(G_FF0, 16, 0, 0, Q_FF0, 2)
            with act.Fori(0, NBLK - 1) as i:
                up_steps(G_FF, 24, i, i + 1, Q_FF, 6)
                for u in range(16, 24):
                    hi(G_FF, 24, i, u + 2)

            def fin_evac(p):
                b = 2 * (p % 2) + 1
                act.wait_ge(fin_turned, p + 1)
                act.activation(out_tm[:, :, (2 * p + 1) * P:(2 * p + 2) * P],
                               aux[:, b, :].rearrange("p (t f) -> p t f", f=P), ACT.Copy).then_inc(fin_out_a, 1)

            for p in range(8):
                if p + 2 < 8:
                    hi(G_FIN, 8, 0, p + 2)
                act.wait_ge(pair_free[p % 2], Q_FIN // 2 + p // 2 + 1)
                if p:
                    act.wait_ge(sq2_added, p)
                act.activation(sq[:, :, :], mixed[:, 2 * p:2 * p + 2, :], ACT.Square).then_inc(sq2_done, 1)
                if p >= 2:
                    act.wait_ge(fin_turned, p - 1)
                for n in range(2):
                    ins = act.activation(x_fin[:, p % 2, n, :], mixed[:, 2 * p + n, :], ACT.Copy,
                                         scale=prm[:, C_NF + 2 * p + n:C_NF + 2 * p + n + 1])
                ins.then_inc(fin_ready, 1)
                if p:
                    fin_evac(p - 1)
            fin_evac(7)
            act.wait_ge(ms2_ready, 1)
            act.activation(rfin[:, :], main[:, 0, 0:4], ACT.Sqrt, bias=eps_t[:, :], scale=1.0 / D).then_inc(rms2_ready, 1)
            act.wait_ge(rfin_ready, 1)
            act.wait_ge(fin_out_v, 8)
            act.wait_ge(fin_out_a, 8)
            for t in (1, 3):
                act.activation(out_tm[:, t, :], out_tm[:, t, :], ACT.Copy, scale=rfin[:, t:t + 1]).then_inc(rows_scaled[1], 1)

        @block.tensor
        def _(pe):
            def triple(dst, slot, cc, n, m_hi_ap, m_lo_ap, start, stop):
                wh = w_hi[:, slot, cc, n * P:n * P + P]
                wl = w_lo[:, slot, cc, n * P:n * P + P]
                pe.matmul(dst, wh, m_hi_ap, start=start, stop=False)
                pe.matmul(dst, wh, m_lo_ap, start=False, stop=False)
                return pe.matmul(dst, wl, m_hi_ap, start=False, stop=stop)

            def unit(base, per, i, u, p, moving, first, last):
                pe.wait_ge(lo_done, splits(base, per, i, u))
                for n in range(2):
                    for cc in range(UC):
                        h, l = moving(cc)
                        ins = triple(main[:, 2 * p + n, :], u % RING, cc, n, h, l,
                                     first and cc == 0, last and cc == UC - 1)
                ins.then_inc(unit_used, 1)

            def u_of(k):
                return lambda cc: (u_hi[:, UC * k + cc, :], u_lo[:, UC * k + cc, :])

            pe.wait_ge(const_landed, 16)
            col = 0
            for r, n in enumerate(PRM_ROWS):
                pe.wait_ge(prm_landed[r], 16 * (3, 5, 5)[r])
                ins = pe.transpose(main[:, 0, col:col + n], prm_rows[0:n, r, :], ident[0:n, 0:n])
                col += n
            ins.then_inc(prm_turned, 1)
            pe.wait_ge(prm_ready, 1)
            for i in range(6):
                if i < 4:
                    pe.wait_ge(tok_landed[i % 2], 16 * (i // 2 + 1))
                    for q in range(4):
                        if i:
                            pe.wait_ge(raw_out, 4 * (i - 1) + q + 1)
                        for a in range(4):
                            ins = pe.transpose(main[:, q, a * P:a * P + P], x_tok[:, i % 2, (4 * q + a) * P:(4 * q + a + 1) * P], ident)
                        ins.then_inc(raw_turned, 1)
                pe.wait_ge(nrm_done, i + 1)
                for q in range(4):
                    if i:
                        pe.wait_ge(nrm_out, 4 * (i - 1) + q + 1)
                    for a in range(4):
                        ins = pe.transpose(aux[:, q, a * P:a * P + P], x_nrm[:, i % 2, (4 * q + a) * P:(4 * q + a + 1) * P], ident)
                    ins.then_inc(nrm_turned, 1)
            pe.wait_ge(cvec_ready, 1)
            pe.wait_ge(raw_out, 16)
            pe.wait_ge(nrm_out, 24)
            with pe.Fori(0, 4) as q:
                for k in range(2):
                    bank = (aux, main)[k]
                    pe.wait_ge(mod_out, q * 2)
                    for j in range(4):
                        pe.wait_ge(ada_landed[j], q * 32 + 16 * k + 16)
                        for cc in range(4):
                            for t in range(4):
                                ins = pe.matmul(bank[:, t, 0:2], ada_pc[:, j, cc, t * P:t * P + P], cvec[:, 4 * j + cc, :],
                                                start=(j == 0 and cc == 0), stop=(j == 3 and cc == 3))
                        ins.then_inc(ada_used, 1)
            pe.wait_ge(mod_out, 8)
            pe.wait_ge(u_lo_done, 32)

            with pe.Fori(0, 2) as i:
                for j in range(2):
                    pe.wait_ge(pair_free[j], i)
                    pe.wait_ge(ctx_free[j], i)
                    for k in range(4):
                        u = 4 * j + k
                        pe.wait_ge(lo_done, splits(G_XA, 8, i, u))
                        for n in range(2):
                            for cc in range(UC):
                                kt = UC * k + cc
                                s, e = kt == 0, kt == KT - 1
                                triple(main[:, 2 * j + n, :], u % RING, cc, n, u_hi[:, kt, :], u_lo[:, kt, :], s, e)
                                ins = triple(aux[:, 2 * j + n, 0:TC], u % RING, cc, n, ctx_hi[:, kt, :], ctx_lo[:, kt, :], s, e)
                        ins.then_inc(unit_used, 1)

            def gates(h, hh, p, d):
                pe.wait_ge(gw_landed[p], hh * 32 + 32)
                pe.wait_ge(conv_done, h + 1)
                if not isinstance(h, int) or h or d:
                    pe.wait_ge(tanh_done, h * 2 + d)
                for ty in range(2):
                    w = gate_w[:, p, ty, d, :]
                    pe.matmul(aux[:, 2 * ty, TC:2 * TC], w, xcv[:, 0:TC], start=True, stop=True)
                    ins = pe.matmul(aux[:, 2 * ty + 1, :], w, xcv[:, TC:TCAT], start=True, stop=True)
                ins.then_inc(gates_done, 1)

            def window(h, hh, p, base, per, i, u0):
                pe.wait_ge(pair_free[p], hh + 2)
                for k in range(4):
                    unit(base, per, i, u0 + k, p, u_of(k), k == 0, k == 3)
                    if k in (1, 2):
                        gates(h, hh, p, k - 1)

            for j in range(2):
                pe.wait_ge(ctx_free[j], 2)
            window(0, 0, 0, G_YX, 4, 0, 0)
            with pe.Fori(0, 3) as i:
                window(i * 2 + 1, i, 1, G_YX + 4, 8, i, 0)
                window(i * 2 + 2, i + 1, 0, G_YX + 4, 8, i, 4)
            window(7, 3, 1, G_YX + 28, 4, 0, 0)

            def channels(t):
                p = (Q_FOUR + t) % 2
                pe.wait_ge(pair_free[p], (Q_FOUR + t) // 2)
                for g in range(4):
                    ins = pe.matmul(main[:, 2 * p + g // 2, (g % 2) * 256:(g % 2) * 256 + 256],
                                    yx[:, 12 + g, t * P:t * P + P], cs128, start=True, stop=True)
                ins.then_inc(chunk_ready, 1)

            def tokens(t):
                p = (Q_FOUR + t) % 2
                pe.wait_ge(dft_landed[t % 3], 16 * (t // 3 + 1))
                pe.wait_ge(pair_free[p], (Q_FOUR + t) // 2 + 1)
                for g in range(4):
                    pe.matmul(aux[:, g, :], xcs[:, t % 2, g, 0:P], dft_t[:, t % 3, 0:T], start=(t == 0), stop=False)
                    ins = pe.matmul(aux[:, g, :], xcs[:, t % 2, g, P:2 * P], dft_t[:, t % 3, T:2 * T], start=False, stop=(t == 3))
                ins.then_inc(chunk_used, 1)

            pe.wait_ge(pair_free[0], 6)
            pe.wait_ge(pair_free[1], 6)
            pe.wait_ge(tanh_done, 16)
            channels(0)
            channels(1)
            tokens(0)
            channels(2)
            tokens(1)
            channels(3)
            tokens(2)
            tokens(3)

            with pe.Fori(0, 8) as i:
                u = 0
                for j, what in enumerate(("g", "pool", "g", "four", "g", "lru")):
                    p = j % 2
                    pe.wait_ge(pair_free[p], i * 3 + (Q_MIX // 2 + j // 2))
                    if what == "g":
                        for k in range(4):
                            unit(G_MIX, 16, i, u, p, u_of(k), k == 0, k == 3)
                            u += 1
                    elif what == "pool":
                        landed(pe, G_MIX, 16, i, u)
                        pe.wait_ge(pool_done, 4)
                        for n in range(2):
                            ins = pe.matmul(main[:, 2 * p + n, :], w_raw[:, u % RING, 0, n * P:n * P + P],
                                            yx[:, ds(i // 2 + 8, 1), :].rearrange("p o n -> p (o n)"), start=True, stop=True)
                        ins.then_inc(unit_used, 1)
                        u += 1
                    elif what == "four":
                        pe.wait_ge(four_lo_done, 4)
                        unit(G_MIX, 16, i, u, p, lambda cc: (four_hi[:, cc, :], four_lo[:, cc, :]), True, True)
                        u += 1
                    else:
                        pe.wait_ge(act_lo, 8)
                        for k in range(2):
                            unit(G_MIX, 16, i, u, p, lambda cc: (act_r[:, UC * k + cc, 0, :], act_r[:, UC * k + cc, 1, :]), k == 0, k == 1)
                            u += 1
                pe.wait_ge(ada2_used[1], i * 8 + 8)
                for t in range(8):
                    ins = pe.matmul(aux[:, 0, ds(i * 8 + t, 1)], ada2_acc[:, t * P:t * P + P], ones[:, 0:1], start=True, stop=True)
                ins.then_inc(acc_used, 1)

            with pe.Fori(0, 4) as i:
                for j in range(2):
                    pe.wait_ge(pair_free[j], i + Q_OUT // 2)
                    for k in range(4):
                        pe.wait_ge(m_lo, UC * k + UC)
                        unit(G_OUT, 8, i, 4 * j + k, j, u_of(k), k == 0, k == 3)
            pe.wait_ge(sq_added, 9)
            pe.matmul(aux[:, 0, :], ones[:, :], sq[:, 0, :], start=True, stop=True).then_inc(ms_ready, 1)

            def up(base, per, i, q0, qi):
                for g in range(4):
                    p = g % 2
                    pe.wait_ge(pair_free[p], q0 // 2 + g // 2 + i * qi)
                    for k in range(4):
                        if base == G_FF0:
                            pe.wait_ge(v_lo, UC * k + UC)
                        unit(base, per, i, 4 * g + k, p, u_of(k), k == 0, k == 3)

            def hid(buf):
                if isinstance(buf, int):
                    return lambda cc: (ff_r[:, buf, 0, cc, :], ff_r[:, buf, 1, cc, :])
                return lambda cc: tuple(ff_r[:, ds(buf, 1), s, cc, :].rearrange("p o n -> p (o n)") for s in range(2))

            up(G_FF0, 16, 0, Q_FF0, 2)
            with pe.Fori(0, NBLK - 1) as i:
                up(G_FF, 24, i, Q_FF, 6)
                pe.wait_ge(hid_lo, i * 2 + 2)
                for j in range(8):
                    pe.wait_ge(pair_free[j % 2], i * 6 + (Q_FF // 2 + 2 + j // 2))
                    unit(G_FF, 24, i, 16 + j, j % 2, hid(i % 2), True, True)

            def turn(p):
                pe.wait_ge(fin_ready, p + 1)
                if p >= 2:
                    pe.wait_ge(fin_out_a, p - 1)
                    pe.wait_ge(fin_out_v, p - 1)
                for n in range(2):
                    for t in range(4):
                        ins = pe.transpose(aux[:, 2 * (p % 2) + n, t * P:t * P + P], x_fin[:, p % 2, n, t * P:t * P + P], ident)
                ins.then_inc(fin_turned, 1)

            pe.wait_ge(hid_lo, 2 * NBLK)
            for j in range(8):
                pe.wait_ge(pair_free[j % 2], Q_FIN // 2 + j // 2)
                unit(G_FIN, 8, 0, j, j % 2, hid((NBLK - 1) % 2), True, True)
                if j:
                    turn(j - 1)
            turn(7)
            pe.wait_ge(sqf2_ready, 1)
            for t in range(4):
                ins = pe.matmul(main[:, 0, t:t + 1], sq[:, 0, t * P:t * P + P], ones[:, 0:1], start=True, stop=True)
            ins.then_inc(ms2_ready, 1)

        @block.vector
        def _(dve):
            chain = Chain(dve, dve_chain)
            link = chain.link

            def lo(base, per, i, u):
                s = u % RING
                dve.wait_ge(hi_done, splits(base, per, i, u))
                dve.tensor_tensor(w_lo[:, s], w_raw[:, s], w_hi[:, s].bitcast(F32), ALU.subtract).then_inc(lo_done, 1)

            dve.memset(ones[:, :], 1.0)
            link(dve.memset(eps_t[:, :], EPS))
            dve.wait_ge(prm_turned, 1)
            dve.tensor_copy(prm[:, :], main[:, 0, 0:NPRM]).then_inc(prm_ready, 1)
            dve.wait_ge(prm_ready, 1)
            for col in (C_BA, C_BX):
                link(dve.tensor_scalar(prm[:, col:col + 16], prm[:, col:col + 16], 0.5, None, ALU.mult))
            lam_p = prm[:, C_LAM:C_LAM + 16]
            link(dve.tensor_scalar(lam[:, 0, :], lam_p, -1.0, None, ALU.mult))
            dve.tensor_tensor(lam[:, 1, :], lam[:, 0, :], lam_p, ALU.min).then_inc(nabs_ready, 1)
            for i in range(6):
                dve.wait_ge(root_done, i + 1)
                dve.wait_ge(tok_landed[i % 2], 16 * (i // 2 + 1))
                link(dve.reciprocal(rstd[:, i:i + 1], rstd[:, i:i + 1]))
                dve.tensor_scalar(x_nrm[:, i % 2, :], x_tok[:, i % 2, :], rstd[:, i:i + 1], None, ALU.mult).then_inc(nrm_done, 1)
                for q in range(4):
                    dve.wait_ge(nrm_turned, 4 * i + q + 1)
                    dst = u_f[:, 4 * q:4 * q + 4, P * i:P * i + P] if i < 4 else ctx_f[:, 4 * q:4 * q + 4, P * (i - 4):P * (i - 3)]
                    dve.tensor_copy(dst, aux[:, q, :].rearrange("p (a b) -> p a b", b=P)).then_inc(nrm_out, 1)
            dve.wait_ge(z_ready, 1)
            z, den, s1, s2, poly = lam[:, 2, :], lam[:, 3, :], lam[:, 3, :], lam[:, 4, :], lam[:, 5, :]
            link(dve.tensor_scalar(den, z, 2.0, None, ALU.add))
            link(dve.reciprocal(den, den))
            link(dve.tensor_tensor(s1, den, z, ALU.mult))
            link(dve.tensor_tensor(s2, s1, s1, ALU.mult))
            link(dve.tensor_scalar(poly, s2, 1.0 / 15, None, ALU.mult))
            for k in (13, 11, 9, 7, 5, 3):
                link(dve.scalar_tensor_tensor(poly, poly, 1.0 / k, s2, ALU.add, ALU.mult))
            link(dve.scalar_tensor_tensor(poly, poly, 1.0, s1, ALU.add, ALU.mult))
            link(dve.tensor_scalar(lam[:, 0, :], lam[:, 0, :], 0.0, None, ALU.max))
            link(dve.scalar_tensor_tensor(poly, poly, 2.0, lam[:, 0, :], ALU.mult, ALU.add))
            dve.tensor_scalar(c2[:, :], poly, 1e-20, -RGLRU_C / 2, ALU.max, ALU.mult).then_inc(c2_ready, 1)
            for u in range(2):
                lo(0, 8, 0, u)
            with dve.Fori(0, 4) as q:
                chain.enter(q, 0, 1)
                for k in range(2):
                    bank = (aux, main)[k]
                    dve.wait_ge(ada_used, q * 8 + 4 * k + 4)
                    for v in range(2):
                        ins = dve.tensor_tensor(mod1[:, v, k, ds(q * 4, 4)], bank[:, :, v],
                                                prm[:, ds(q * 4 + (C_BADA + 16 * k), 4)], ALU.add)
                    ins.then_inc(mod_out, 1)
                dve.wait_ge(mod_out, q * 2 + 2)
                dve.scalar_tensor_tensor(gsc1[:, 0, ds(q * 4, 4)], mod1[:, 0, 1, ds(q * 4, 4)], 1.0,
                                         prm[:, ds(q * 4 + C_N1, 4)], ALU.add, ALU.mult)
                link(dve.scalar_tensor_tensor(gsc1[:, 1, ds(q * 4, 4)], mod1[:, 1, 1, ds(q * 4, 4)], 1.0,
                                              prm[:, ds(q * 4 + C_N1, 4)], ALU.add, ALU.mult))
                for t in range(4):
                    k = ds(q * 4 + t, 1)
                    for v, f in enumerate((u_f, ctx_f)):
                        dve.tensor_scalar(f[:, k, :], f[:, k, :], gsc1[:, v, k], mod1[:, v, 0, k],
                                          ALU.mult, ALU.add).then_inc(u_aff, 1)
                for t in range(4):
                    k = ds(q * 4 + t, 1)
                    for v, (f, l, h) in enumerate(((u_f, u_lo, u_hi), (ctx_f, ctx_lo, ctx_hi))):
                        dve.wait_ge(u_hi_done, q * 8 + 2 * t + v + 1)
                        dve.tensor_tensor(l[:, k, :], f[:, k, :], h[:, k, :].bitcast(F32), ALU.subtract).then_inc(u_lo_done, 1)
                chain.leave(4)

            dve.wait_ge(ada_used, 32)
            dve.memset(pad[:, :, 0:2], 0.0)
            dve.memset(pad[:, :, 2 + TC:PADX], 0.0)
            link(dve.memset(pad[:, :, PADX + T:PADX + T + 1], 0.0))
            with dve.Fori(0, 2) as i:
                for u in range(8):
                    lo(G_XA, 8, i, u + 2)
                    if u % 4 == 3:
                        j = u // 4
                        dve.wait_ge(unit_used, i * 8 + u + 1)
                        dve.tensor_copy(pad[:, ds(i * 4 + 2 * j, 2), 2:2 + TC], aux[:, 2 * j:2 * j + 2, 0:TC]).then_inc(ctx_free[j], 1)

            def conv(h):
                row = ds(h, 1)

                def tap(k):
                    return prm[:, ds(h + (C_CW + 8 * k), 1)]

                for k in range(4):
                    for a, b, n in ((0, 0, TC), (TC, PADX - 2, T)):
                        src = pad[:, row, b + k:b + k + n].rearrange("p o n -> p (o n)")
                        dst = xcv[:, a:a + n]
                        if k == 0:
                            ins = dve.tensor_scalar(dst, src, tap(0), prm[:, ds(h + C_CB, 1)], ALU.mult, ALU.add)
                        else:
                            ins = dve.scalar_tensor_tensor(dst, src, tap(k), dst, ALU.mult, ALU.add)
                    if k < 3:
                        link(ins)
                ins.then_inc(conv_done, 1)

            def mid(h):
                for d in range(2):
                    dve.wait_ge(decay_done, h * 2 + d + 1)
                    link(dve.tensor_scalar(ld[:, :], lt[:, d, :], -1.0, 1.0, ALU.mult, ALU.add))
                    link(dve.reciprocal(ld[:, :], ld[:, :]))
                    dve.scalar_tensor_tensor(lt[:, d, :], lt[:, d, :], -0.5, ld[:, :], ALU.mult, ALU.mult).then_inc(q_done, 1)
                    link(dve.scalar_tensor_tensor(lb[:, d, :], lb[:, d, :], 1.0, xcv[:, :], ALU.add, ALU.mult))

            def final(h):
                for d in range(2):
                    dve.wait_ge(root_q, h * 2 + d + 1)
                    link(dve.tensor_tensor(lb[:, d, :], lb[:, d, :], lt[:, d, :], ALU.mult))
                    a_c, b_c, s_c = la[:, d, 0:TC], lb[:, d, 0:TC], lcs[:, :]
                    a_x, b_x, s_x = la[:, d, TC:TCAT], lb[:, d, TC:TCAT], lh[:, d, :]
                    end = lcs[:, TC - 1:TC]
                    if d:
                        a_c, b_c, s_c, a_x, b_x, s_x = (v[:, ::-1] for v in (a_c, b_c, s_c, a_x, b_x, s_x))
                        end = lcs[:, 0:1]
                    link(dve.tensor_tensor_scan(s_c, a_c, b_c, 0.0, ALU.mult, ALU.add))
                    link(dve.tensor_tensor_scan(s_x, a_x, b_x, end, ALU.mult, ALU.add))
                dve.tensor_tensor(pad[:, ds(h, 1), 0:T].rearrange("p o n -> p (o n)"), lh[:, 0, :], lh[:, 1, :], ALU.add).then_inc(lru_done, 1)

            def window(h, base, per, i, u0, first=False):
                for u in range(4):
                    lo(base, per, i, u0 + u + 2)
                    if u == 0:
                        if not first:
                            mid(h - 1)
                        conv(h)
                    if u == 1 and not first:
                        final(h - 1)

            for j in range(2):
                dve.wait_ge(pair_free[j], 2)
                dve.wait_ge(ctx_free[j], 2)
            window(0, G_YX, 4, 0, 0, first=True)
            with dve.Fori(0, 3) as i:
                chain.enter(i, 0, 30)
                window(i * 2 + 1, G_YX + 4, 8, i, 0)
                window(i * 2 + 2, G_YX + 4, 8, i, 4)
                chain.leave(3)
            window(7, G_YX + 28, 4, 0, 0)
            mid(7)
            final(7)

            dve.wait_ge(lru_done, 8)
            dve.memset(pw_a[:, :, 0:8], 0.0)
            link(dve.memset(pw_a[:, :, 72:80], 0.0))
            dve.wait_ge(pair_free[0], 6)
            for g in range(4):
                xb = yx[:, 8 + g, :].rearrange("p (r w) -> p r w", w=GRID_W)
                if g:
                    dve.wait_ge(pool_done, g)
                    dve.memset(pw_a[:, :, 0:8], 0.0)
                    dve.memset(pw_a[:, :, 72:80], 0.0)
                link(dve.tensor_copy(pw_a[:, :, 8:72], xb))
                src, dst, n = pw_a, pw_b, 80
                for k in range(g + 1):
                    n -= 1 << k
                    link(dve.tensor_tensor(dst[:, :, 0:n], src[:, :, 0:n], src[:, :, (1 << k):(1 << k) + n], ALU.add))
                    src, dst = dst, src
                half = 1 << g
                mean = dst[:, :, 0:GRID_W]
                cnt = inv_cnt[:, GRID_W * g:GRID_W * (g + 1)].unsqueeze(1).to_broadcast([P, ROWS, GRID_W])
                link(dve.tensor_tensor(mean, src[:, :, 8 - half:8 - half + GRID_W], cnt, ALU.mult))
                dve.tensor_tensor(xb, mean, xb, ALU.subtract).then_inc(pool_done, 1)
            for g in range(4):
                dve.wait_ge(four_hi_done, g + 1)
                dve.tensor_tensor(four_lo[:, g, :], aux[:, g, :], four_hi[:, g, :].bitcast(F32), ALU.subtract).then_inc(four_lo_done, 1)
            dve.wait_ge(lru_done, 8)
            for h in range(HEADS):
                dve.wait_ge(gelu_done, h + 1)
                dve.tensor_tensor(act_f[:, h, 1, :], pad[:, h, 0:T], yx[:, h, :], ALU.mult).then_inc(prod_done, 1)
            for h in range(HEADS):
                dve.wait_ge(act_hi, h + 1)
                dve.tensor_tensor(act_r[:, h, 1, :], act_f[:, h, 1, :], act_r[:, h, 0, :].bitcast(F32), ALU.subtract).then_inc(act_lo, 1)

            with dve.Fori(0, 8) as i:
                dst = mixed[:, ds(i * 2, 2), :]
                for u in range(16):
                    if u + 2 != POOL_AT:
                        lo(G_MIX, 16, i, u + 2)
                    s = u % 2
                    dve.wait_ge(ada2_landed[s], i * 128 + 16 * (u // 2 + 1))
                    if u == 0:
                        dve.wait_ge(acc_used, i)
                        ins = dve.tensor_scalar(ada2_acc[:, :], ada2_pc[:, s, :], cvec[:, u, 0:1], None, ALU.mult)
                    else:
                        dve.wait_ge(ada2_used[1 - s], i * 8 + (u + 1) // 2)
                        ins = dve.scalar_tensor_tensor(ada2_acc[:, :], ada2_pc[:, s, :], cvec[:, u, 0:1],
                                                       ada2_acc[:, :], ALU.mult, ALU.add)
                    ins.then_inc(ada2_used[s], 1)
                    if u in (4, 9, 15):
                        k = (4, 9, 15).index(u)
                        dve.wait_ge(unit_used, i * 16 + (G_MIX + u + 1))
                        dve.wait_ge(pair_free[0], i * 3 + (Q_MIX // 2 + k + 1))
                        if k == 0:
                            for n in range(2):
                                ins = dve.scalar_tensor_tensor(mixed[:, ds(i * 2 + n, 1), :].rearrange("p o n -> p (o n)"),
                                                               main[:, 2 + n, :], prm[:, ds(i * 2 + (C_PS + n), 1)],
                                                               gate[:, n, :], ALU.mult, ALU.mult)
                            ins.then_inc(pair_free[1], 1)
                        else:
                            dve.tensor_tensor(gate[:, :, :], main[:, 2:4, :], gate[:, :, :], ALU.mult).then_inc(pair_free[1], 1)
                            dve.wait_ge(pair_free[1], i * 3 + (Q_MIX // 2 + k + 1))
                            if k == 2:
                                dve.wait_ge(gate_used, i * 2 + 1)
                            dve.tensor_tensor(dst, dst, gate[:, :, :], ALU.add).then_inc(gate_used, 1)
            dve.wait_ge(acc_used, 8)
            link(dve.tensor_tensor(mod2[:, :], aux[:, 0, 0:64], prm[:, C_BADA + 32:C_BADA + 96], ALU.add))
            dve.scalar_tensor_tensor(gsc2[:, :], mod2[:, 32:48], 1.0, prm[:, C_N2:C_N2 + 16], ALU.add, ALU.mult)
            link(dve.memset(sq_acc[:, :, :], 0.0))
            dve.wait_ge(gate_used, 16)
            for k in range(KT):
                dve.wait_ge(m_hi, k + 1)
                dve.tensor_tensor(u_lo[:, k, :], mixed[:, k, :], u_hi[:, k, :].bitcast(F32), ALU.subtract).then_inc(m_lo, 1)

            with dve.Fori(0, 4) as i:
                for u in range(8):
                    lo(G_OUT, 8, i, u + 2)
                    if u % 4 == 3:
                        j = u // 4
                        dve.wait_ge(unit_used, i * 8 + (G_OUT + u + 1))
                        dve.wait_ge(res_landed[j], i * 16 + 16)
                        for n in range(2):
                            ins = dve.scalar_tensor_tensor(mixed[:, ds(i * 4 + (2 * j + n), 1), :].rearrange("p o n -> p (o n)"),
                                                           main[:, 2 * j + n, :], mod2[:, ds(i * 4 + (2 * j + n), 1)],
                                                           x_res[:, j, n, :], ALU.mult, ALU.add)
                        ins.then_inc(pair_free[j], 1)
                        dve.wait_ge(sq_done, i * 2 + j + 1)
                        dve.wait_ge(sq_added, i * 2 + j)
                        dve.tensor_tensor(sq_acc[:, :, :], sq_acc[:, :, :], sq[:, :, :], ALU.add).then_inc(sq_added, 1)
            dve.wait_ge(sq_added, 8)
            dve.tensor_tensor(sq[:, 0, :], sq_acc[:, 0, :], sq_acc[:, 1, :], ALU.add).then_inc(sq_added, 1)
            dve.wait_ge(rms_ready, 1)
            link(dve.reciprocal(rstd_b[:, :], rstd_b[:, :]))
            with dve.Fori(0, 4) as q:
                chain.enter(q, 0, 1)
                for t in range(4):
                    k = ds(q * 4 + t, 1)
                    ins = dve.tensor_tensor(u_f[:, k, :].rearrange("p o n -> p (o n)"),
                                            mixed[:, k, :].rearrange("p o n -> p (o n)"), rstd_b[:, :], ALU.mult)
                link(ins)
                for t in range(4):
                    k = ds(q * 4 + t, 1)
                    dve.tensor_scalar(u_f[:, k, :], u_f[:, k, :], gsc2[:, k], mod2[:, ds(q * 4 + (16 + t), 1)],
                                      ALU.mult, ALU.add).then_inc(v_aff, 1)
                for t in range(4):
                    k = ds(q * 4 + t, 1)
                    dve.wait_ge(v_hi, q * 4 + t + 1)
                    dve.tensor_tensor(u_lo[:, k, :], u_f[:, k, :], u_hi[:, k, :].bitcast(F32), ALU.subtract).then_inc(v_lo, 1)
                chain.leave(4)

            def up_steps(base, per, i, b, q0, qi):
                for u in range(16):
                    lo(base, per, i, u + 2)
                    if u % 8 == 7:
                        pr = u // 8
                        pos = ds(b % 2, 1) if not isinstance(b, int) else slice(b % 2, b % 2 + 1)
                        cols = slice(2 * pr, 2 * pr + 2)
                        f = ff_f[:, pos, 1, cols, :].rearrange("p o a n -> p (o a) n")
                        l = ff_r[:, pos, 1, cols, :].rearrange("p o a n -> p (o a) n")
                        h = ff_r[:, pos, 0, cols, :].rearrange("p o a n -> p (o a) n").bitcast(F32)
                        dve.wait_ge(unit_used, base + u + 1 + i * per)
                        dve.wait_ge(pair_free[0], q0 // 2 + pr + 1 + i * qi)
                        dve.tensor_tensor(f, gate[:, :, :], main[:, 2:4, :], ALU.mult).then_inc(pair_free[1], 1)
                        dve.wait_ge(hid_hi, b * 2 + pr + 1)
                        dve.tensor_tensor(l, f, h, ALU.subtract).then_inc(hid_lo, 1)

            def down_add(p, j):
                for n in range(2):
                    k = 2 * j + n
                    ins = dve.scalar_tensor_tensor(mixed[:, k, :], main[:, 2 * p + n, :], mod2[:, 48 + k:49 + k],
                                                   mixed[:, k, :], ALU.mult, ALU.add)
                ins.then_inc(pair_free[p], 1)

            up_steps(G_FF0, 16, 0, 0, Q_FF0, 2)
            with dve.Fori(0, NBLK - 1) as i:
                up_steps(G_FF, 24, i, i + 1, Q_FF, 6)
                for j in range(8):
                    lo(G_FF, 24, i, 16 + j + 2)
                    dve.wait_ge(unit_used, i * 24 + (G_FF + 16 + j + 1))
                    down_add(j % 2, j)

            def fin_evac(p):
                b = 2 * (p % 2)
                dve.wait_ge(fin_turned, p + 1)
                dve.tensor_copy(out_tm[:, :, 2 * p * P:(2 * p + 1) * P],
                                aux[:, b, :].rearrange("p (t f) -> p t f", f=P)).then_inc(fin_out_v, 1)

            link(dve.memset(sq_acc[:, :, :], 0.0))
            for p in range(8):
                if p + 2 < 8:
                    lo(G_FIN, 8, 0, p + 2)
                dve.wait_ge(unit_used, G_FIN + p + 1)
                down_add(p % 2, p)
                dve.wait_ge(sq2_done, p + 1)
                if p:
                    dve.wait_ge(sq2_added, p)
                dve.tensor_tensor(sq_acc[:, :, :], sq_acc[:, :, :], sq[:, :, :], ALU.add).then_inc(sq2_added, 1)
                if p:
                    fin_evac(p - 1)
            dve.wait_ge(sq2_added, 8)
            dve.tensor_tensor(sq[:, 0, :], sq_acc[:, 0, :], sq_acc[:, 1, :], ALU.add).then_inc(sqf2_ready, 1)
            fin_evac(7)
            dve.wait_ge(rms2_ready, 1)
            dve.reciprocal(rfin[:, :], rfin[:, :]).then_inc(rfin_ready, 1)
            dve.wait_ge(rfin_ready, 1)
            dve.wait_ge(fin_out_a, 8)
            dve.wait_ge(fin_out_v, 8)
            for t in (0, 2):
                dve.tensor_scalar(out_tm[:, t, :], out_tm[:, t, :], rfin[:, t:t + 1], None, ALU.mult).then_inc(rows_scaled[0], 1)


_INS = ["x", "c", "ctx", "c_ctx", "w_ada", "b_ada", "norm1_g", "norm2_g", "w_in", "conv_w", "conv_b",
        "lru_wa", "lru_ba", "lru_wx", "lru_bx", "lru_lambda", "w_lru_out", "w_pool", "pool_scale",
        "w_fourier", "b_gate", "w_out", "w_ffn_in", "w_ffn_out", "norm_f_g"]


def shape_tables():
    def wave(n):
        angle = 2 * np.pi * (np.outer(np.arange(n), np.arange(n)) % n) / n
        return np.cos(angle), np.sin(angle)

    c_ch, s_ch = wave(P)
    t = np.arange(GRID_W)
    counts = []
    for w in (2, 4, 8, 16):
        low, high = np.clip(t - w // 2, 0, GRID_W), np.clip(t - w // 2 + w, 0, GRID_W)
        counts.append(1.0 / (high - low))
    counts = np.tile(np.concatenate(counts)[None, :], (P, 1))
    consts = np.concatenate([np.eye(P), c_ch, s_ch, counts], axis=1).astype(np.float32)
    c_tok, s_tok = wave(T)
    norm = 1.0 / np.sqrt(T * P)
    dft = np.concatenate([c_tok * norm, -s_tok * norm], axis=1).astype(np.float32)
    return consts, dft.reshape(T // P, P, 2 * T)


def kernel(**inputs):
    import concourse.bacc as bacc
    from concourse.bass_utils import run_bass_kernel_spmd

    nc = bacc.Bacc("TRN2", target_bir_lowering=False, num_devices=1, dynamic_dma_scratch_size=1024)
    arrays, args = {}, []

    def feed(name, a):
        a = np.ascontiguousarray(a)
        arrays[name] = a
        args.append(nc.dram_tensor(name, a.shape, mybir.dt.from_np(a.dtype), kind="ExternalInput").ap())

    for name in _INS:
        feed(f"in_{name}", inputs[name])
    consts, dft = shape_tables()
    feed("in_consts", consts)
    feed("in_dft", dft)
    args.append(nc.dram_tensor("out_x", (1, T, D), F32, kind="ExternalOutput").ap())
    args.append(nc.dram_tensor("x_feature_major", (P, KT, T), F32, kind="Internal").ap())
    build(nc, *args)
    result = run_bass_kernel_spmd(nc, [arrays], core_ids=[0])
    return result.results[0]["out_x"]
```

```python
from contextlib import ExitStack

import numpy as np

import concourse.bass as bass
from concourse import mybir

F32 = mybir.dt.float32
F32R = mybir.dt.float32r
ALU = mybir.AluOpType
ACT = mybir.ActivationFunctionType
ds = bass.ds

P = 128
D = 2048
T = 512
TC = 256
KT = D // P
GRID_W = 64
ROWS = T // GRID_W
D_LRU = D // 2
HEADS = D_LRU // P
I_YA, I_XB, I_G = D_LRU, 2 * D_LRU, 2 * D_LRU + D // 2
D_FF = ((8 * D + 3 * 256 - 1) // (3 * 256)) * 256
EPS = 1e-6
RGLRU_C = 8.0
TCAT = TC + T
PADX = TC + 5

NCOS = T // 2 + 1
RING = 4
UC = 4
UN = 256

NBLK = D_FF // (4 * P)
G_XA = 0
G_YX = G_XA + 16
G_MIX = G_YX + 32
G_OUT = G_MIX + 128
G_FF0 = G_OUT + 32
G_FF = G_FF0 + 16
G_FIN = G_FF + 24 * (NBLK - 1)
G_END = G_FIN + 8
POOL_AT = 4

Q_YX = 4
Q_FOUR = Q_YX + 8
Q_MIX = Q_FOUR + 4
Q_OUT = Q_MIX + 48
Q_FF0 = Q_OUT + 8
Q_FF = Q_FF0 + 4
Q_FIN = Q_FF + 12 * (NBLK - 1)

C_BADA, C_N1, C_N2 = 0, 96, 112
C_BG, C_PS, C_CW, C_CB, C_NF = 128, 176, 192, 224, 232
C_BA, C_BX, C_LAM, C_C, C_CC = 248, 264, 280, 296, 312
NPRM = 328
PRM_ROWS = (128, 120, 80)


class Chain:

    def __init__(self, eng, sem):
        self.eng, self.sem, self.n, self.shift = eng, sem, 0, 0

    def link(self, ins):
        self.n += 1
        ins.then_inc(self.sem, 1)
        self.eng.wait_ge(self.sem, self.n + self.shift)

    def enter(self, i, start, per):
        self.at, self.per = self.n, per
        self.shift = (i - start) * per

    def leave(self, times):
        assert self.n - self.at == self.per, (self.n - self.at, self.per)
        self.n, self.shift = self.at + self.per * times, 0


def build(nc, x, c, ctx_in, c_ctx, w_ada, b_ada, norm1_g, norm2_g, w_in, conv_w, conv_b, lru_wa, lru_ba,
          lru_wx, lru_bx, lru_lambda, w_lru_out, w_pool, pool_scale, w_fourier, b_gate, w_out,
          w_ffn_in, w_ffn_out, norm_f_g, consts, dft, out, x_fm):
    with ExitStack() as stack:
        kb = 1024
        at = 1152
        where = {}
        for region, size in (("raw", 16 * kb), ("hi", 16 * kb), ("u_hi", 32 * kb), ("u_lo", 32 * kb),
                             ("mix", 32 * kb), ("lru", 32 * kb), ("yx", 32 * kb), ("pf", 8 * kb),
                             ("gate", 4 * kb), ("ada", 12 * kb), ("misc", 5952)):
            where[region] = at
            at += size
        assert at <= nc.sbuf_usable_end, (at, nc.sbuf_usable_end)
        misc_at = [where["misc"]]

        def sb(name, region, shape, dt=F32, off=0):
            return nc.alloc_sbuf_tensor_at(name, [P, *shape], dt, offset=where[region] + off)

        def misc(name, shape):
            t = nc.alloc_sbuf_tensor_at(name, [P, *shape], F32, offset=misc_at[0])
            misc_at[0] += (4 * int(np.prod(shape)) + 31) // 32 * 32
            assert misc_at[0] <= where["misc"] + 5952, misc_at[0] - where["misc"]
            return t

        w_raw = sb("w_raw", "raw", [RING, UC, UN])
        w_lo = sb("w_lo", "raw", [RING, UC, UN], F32R)
        w_hi = sb("w_hi", "hi", [RING, UC, UN], F32R)
        u_hi = sb("u_hi", "u_hi", [KT, T], F32R)
        u_f = sb("u_f", "u_lo", [KT, T])
        u_lo = sb("u_lo", "u_lo", [KT, T], F32R)
        out_tm = sb("out_tm", "u_hi", [4, D])
        ctx_hi = sb("ctx_hi", "mix", [KT, TC], F32R)
        ctx_f = sb("ctx_f", "mix", [KT, TC], F32, 16 * kb)
        ctx_lo = sb("ctx_lo", "mix", [KT, TC], F32R, 16 * kb)
        x_stage = sb("x_stage", "mix", [2, KT, P])
        prm_rows = sb("prm_rows", "mix", [3, P], F32, 16 * kb)
        xcv = sb("xcv", "mix", [TCAT])
        la = sb("la", "mix", [2, TCAT], F32, 3 * kb)
        lb = sb("lb", "mix", [2, TCAT], F32, 9 * kb)
        lt = sb("lt", "mix", [2, TCAT], F32, 15 * kb)
        ld = sb("ld", "mix", [TCAT], F32, 21 * kb)
        lcs = sb("lcs", "mix", [TC], F32, 24 * kb)
        lh = sb("lh", "mix", [2, T], F32, 25 * kb)
        pw_a = sb("pw_a", "mix", [ROWS, 80], F32, 29 * kb)
        pw_b = sb("pw_b", "ada", [ROWS, 80], F32, 8 * kb)
        mixed = sb("mixed", "mix", [KT, T])
        ada_pc = sb("ada_pc", "lru", [4, 4, 512])
        pad = sb("pad", "lru", [HEADS, 1024])
        act_f = sb("act_f", "lru", [HEADS, 2, T])
        act_r = sb("act_r", "lru", [HEADS, 2, T], F32R)
        ff_f = sb("ff_f", "lru", [2, 2, 4, T])
        ff_r = sb("ff_r", "lru", [2, 2, 4, T], F32R)
        yx = sb("yx", "yx", [KT, T])
        four_f = sb("four_f", "yx", [4, T], F32, 24 * kb)
        four_lo = sb("four_lo", "yx", [4, T], F32R, 24 * kb)
        four_hi = sb("four_hi", "pf", [4, T], F32R)
        x_tok = sb("x_tok", "yx", [2, D])
        x_nrm = sb("x_nrm", "yx", [2, D], F32, 16 * kb)
        xcs = sb("xcs", "pf", [2, 4, 256])
        sq = sb("sq", "pf", [2, T])
        sq_acc = sb("sq_acc", "pf", [2, T], F32, 4 * kb)
        rstd_b = sb("rstd_b", "pf", [T])
        gate = sb("gate", "gate", [2, T])
        ada_row = sb("ada_row", "gate", [2, T])
        gate_w = sb("gate_w", "gate", [2, 2, 2, P])
        dft_t = sb("dft_t", "ada", [4, T])
        ada2_pc = sb("ada2_pc", "ada", [2, 1024])
        ada2_acc = sb("ada2_acc", "ada", [1024], F32, 8 * kb)
        x_res = sb("x_res", "ada", [2, 2, T])
        x_fin = sb("x_fin", "ada", [2, 2, T])

        const = misc("const", [640])
        ident, cs128, inv_cnt = const[:, 0:128], const[:, 128:384], const[:, 384:640]
        ones = misc("ones", [P])
        prm = misc("prm", [NPRM])
        cvec = misc("cvec", [KT, 2])
        mod1 = misc("mod1", [2, 2, KT])
        gsc1 = misc("gsc1", [2, KT])
        mod2 = misc("mod2", [64])
        gsc2 = misc("gsc2", [KT])
        c2 = misc("c2", [16])
        lam = misc("lam", [6, 16])
        ssum = misc("ssum", [6])
        rstd = misc("rstd", [6])
        rfin = misc("rfin", [4])
        eps_t = misc("eps_t", [1])
        spare = misc("spare", [1])

        main = stack.enter_context(nc.psum_tensor("main", [P, 4, 512], F32))
        aux = stack.enter_context(nc.psum_tensor("aux", [P, 4, 512], F32))
        aux_flat = aux[:, :, :].rearrange("p b n -> p (b n)")

        def sem(name):
            return stack.enter_context(nc.semaphore(name))

        unit_landed = [sem(f"unit_landed{s}") for s in range(RING)]
        const_landed = sem("const_landed")
        prm_landed = [sem(f"prm_landed{r}") for r in range(3)]
        tok_landed = [sem(f"tok_landed{s}") for s in range(2)]
        ada_landed = [sem(f"ada_landed{s}") for s in range(4)]
        gw_landed = [sem(f"gw_landed{s}") for s in range(2)]
        dft_landed = [sem(f"dft_landed{s}") for s in range(4)]
        ada2_landed = [sem(f"ada2_landed{s}") for s in range(2)]
        res_landed = [sem(f"res_landed{s}") for s in range(2)]
        x_stored = [sem(f"x_stored{s}") for s in range(2)]
        out_stored = sem("out_stored")
        hi_done, lo_done, unit_used = sem("hi_done"), sem("lo_done"), sem("unit_used")
        pair_free = [sem("pair_free0"), sem("pair_free1")]
        ctx_free = [sem("ctx_free0"), sem("ctx_free1")]
        act_chain, dve_chain, pool_chain = sem("act_chain"), sem("dve_chain"), sem("pool_chain")
        ones_set, prm_turned, prm_ready = sem("ones_set"), sem("prm_turned"), sem("prm_ready")
        cvec_ready = sem("cvec_ready")
        root_done, nrm_done = sem("root_done"), sem("nrm_done")
        raw_turned, raw_out = sem("raw_turned"), sem("raw_out")
        nrm_turned, nrm_out = sem("nrm_turned"), sem("nrm_out")
        ada_used, row_out, row_turned, mod_out = sem("ada_used"), sem("row_out"), sem("row_turned"), sem("mod_out")
        u_aff, u_hi_done, u_lo_done = sem("u_aff"), sem("u_hi_done"), sem("u_lo_done")
        nabs_ready, z_ready, c2_ready = sem("nabs_ready"), sem("z_ready"), sem("c2_ready")
        conv_done, gates_done, decay_done = sem("conv_done"), sem("gates_done"), sem("decay_done")
        tanh_done = sem("tanh_done")
        gated = sem("gated")
        q_done, root_q, lru_done = sem("q_done"), sem("root_q"), sem("lru_done")
        gelu_done, prod_done, act_hi, act_lo = sem("gelu_done"), sem("prod_done"), sem("act_hi"), sem("act_lo")
        chunk_ready, four_done = sem("chunk_ready"), sem("four_done")
        chunk_used, four_hi_done, four_lo_done = sem("chunk_used"), sem("four_hi_done"), sem("four_lo_done")
        pool_done = sem("pool_done")
        gate_used = sem("gate_used")
        ada2_used = [sem("ada2_used0"), sem("ada2_used1")]
        acc_used = sem("acc_used")
        m_hi, m_lo = sem("m_hi"), sem("m_lo")
        sq_done, sq_added, ms_ready = sem("sq_done"), sem("sq_added"), sem("ms_ready")
        rms_ready, v_aff, v_hi, v_lo = sem("rms_ready"), sem("v_aff"), sem("v_hi"), sem("v_lo")
        hid_hi, hid_lo = sem("hid_hi"), sem("hid_lo")
        sq2_done, sq2_added = sem("sq2_done"), sem("sq2_added")
        fin_ready, fin_turned = sem("fin_ready"), sem("fin_turned")
        fin_out_a, fin_out_v = sem("fin_out_a"), sem("fin_out_v")
        sqf2_ready, ms2_ready, rms2_ready, rfin_ready = sem("sqf2_ready"), sem("ms2_ready"), sem("rms2_ready"), sem("rfin_ready")
        rows_scaled = [sem("rows_scaled_v"), sem("rows_scaled_a")]

        def landed(eng, base, per, i, u):
            eng.wait_ge(unit_landed[u % RING], (base // RING + u // RING + 1) * 16 + i * (16 * per // RING))

        def splits(base, per, i, u):
            if base < G_MIX:
                return base + u + 1 + i * per
            if base == G_MIX:
                return base + u + 1 - (u > POOL_AT) + i * (per - 1)
            return base + u + 1 - 8 + i * per

        in_t = w_in[0].rearrange("(c p) n -> p c n", p=P)
        ada_t = w_ada[0].rearrange("(c p) n -> p c n", p=P)
        lru_t = w_lru_out[0].rearrange("(c p) (g n) -> p c g n", p=P, n=2 * UN)
        four_t = w_fourier[0].rearrange("(c p) (g n) -> p c g n", p=P, n=2 * UN)
        pool_t = w_pool[0].rearrange("g p n -> p g n")
        out_t = w_out[0].rearrange("(c p) n -> p c n", p=P)
        ffi_t = w_ffn_in[0].rearrange("(c p) n -> p c n", p=P)
        ffo_t = w_ffn_out[0].rearrange("(c p) n -> p c n", p=P)

        block = stack.enter_context(nc.Block())

        @block.sync
        def _(sp):
            def unit(base, per, i, u, src, raw_only=False):
                if not (base == 0 and u < RING and isinstance(i, int) and i == 0):
                    sp.wait_ge(unit_used, base + u - RING + 1 + i * per)
                dst = w_raw[:, u % RING, 0, :] if raw_only else w_raw[:, u % RING, :, :]
                sp.dma_start(dst, src).then_inc(unit_landed[u % RING], 16)

            def ada_piece(col, j, used):
                if used is not None:
                    sp.wait_ge(ada_used, used)
                sp.dma_start(ada_pc[:, j, :, :], ada_t[:, 4 * j:4 * j + 4, col]).then_inc(ada_landed[j], 16)

            sp.dma_start(const[:, :], consts).then_inc(const_landed, 16)
            toks = [x[0, P * i:P * i + P, :] for i in range(4)] + [ctx_in[0, P * i:P * i + P, :] for i in range(2)]
            for i in range(2):
                if i:
                    sp.wait_ge(prm_landed[2], 80)
                sp.dma_start(x_tok[:, i, :], toks[i]).then_inc(tok_landed[i], 16)
            for j in range(4):
                ada_piece(slice(0, 512), j, None)
            for i in range(6):
                if i < 4:
                    sp.wait_ge(raw_out, 4 * (i + 1))
                    sp.dma_start(x_fm[:, :, P * i:P * i + P], x_stage[:, i % 2, :, :]).then_inc(x_stored[i % 2], 16)
                if i + 2 < 6:
                    sp.wait_ge(nrm_done, i + 1)
                    sp.wait_ge(raw_turned, 4 * min(i + 1, 4))
                    sp.dma_start(x_tok[:, i % 2, :], toks[i + 2]).then_inc(tok_landed[i % 2], 16)
                if i < 4:
                    ada_piece(slice(D, D + 512), i, i + 1)
            for u in range(RING):
                unit(0, 8, 0, u, in_t[:, UC * u:UC * u + UC, 0:UN])
            with sp.Fori(1, 4) as q:
                for k in range(2):
                    for j in range(4):
                        ada_piece(ds(q * 512 + D * k, 512), j, q * 8 + (4 * k + j - 3))
            with sp.Fori(1, 4) as i:
                for u in range(4):
                    unit(G_XA, 4, i, u, in_t[:, UC * u:UC * u + UC, ds(i * UN, UN)])

            def window(h, hh, p, base, per, i, u0):
                if not isinstance(h, int) or h >= 2:
                    sp.wait_ge(gates_done, h * 2 - 2)
                sp.dma_start(gate_w[:, p, 0, :, :], lru_wa[0][:, ds(h, 1), :, :].rearrange("d h i j -> (h i) d j")).then_inc(gw_landed[p], 16)
                sp.dma_start(gate_w[:, p, 1, :, :], lru_wx[0][:, ds(h, 1), :, :].rearrange("d h i j -> (h i) d j")).then_inc(gw_landed[p], 16)
                for u in range(4):
                    unit(base, per, i, u0 + u, in_t[:, UC * u:UC * u + UC, ds(h * UN + I_YA, UN)])

            window(0, 0, 0, G_YX, 4, 0, 0)
            with sp.Fori(0, 3) as i:
                window(i * 2 + 1, i, 1, G_YX + 4, 8, i, 0)
                window(i * 2 + 2, i + 1, 0, G_YX + 4, 8, i, 4)
            window(7, 3, 1, G_YX + 28, 4, 0, 0)
            for t in range(4):
                sp.dma_start(dft_t[:, t, :], dft[t]).then_inc(dft_landed[t], 16)

            with sp.Fori(0, 8) as i:
                def gcols(branch):
                    return ds(i * UN + (I_G + branch * D), UN)
                u = 0
                for what in ("pool", "four", "lru"):
                    for k in range(4):
                        unit(G_MIX, 16, i, u, in_t[:, UC * k:UC * k + UC, gcols(("lru", "pool", "four").index(what))])
                        u += 1
                    if what == "pool":
                        unit(G_MIX, 16, i, u, pool_t[:, ds(i // 2, 1), ds((i % 2) * UN, UN)].rearrange("p g n -> p (g n)"), raw_only=True)
                        u += 1
                    elif what == "four":
                        src = four_t[:, :, ds(i // 2, 1), ds((i % 2) * UN, UN)]
                        unit(G_MIX, 16, i, u, src.rearrange("p c g n -> p c (g n)"))
                        u += 1
                    else:
                        for k in range(2):
                            src = lru_t[:, UC * k:UC * k + UC, ds(i // 2, 1), ds((i % 2) * UN, UN)]
                            unit(G_MIX, 16, i, u, src.rearrange("p c g n -> p c (g n)"))
                            u += 1

            with sp.Fori(0, 4) as i:
                for j in range(2):
                    for k in range(4):
                        unit(G_OUT, 8, i, 4 * j + k, out_t[:, UC * k:UC * k + UC, ds((i * 2 + j) * UN, UN)])
                        if k == 1:
                            sp.wait_ge(ada2_used[j], 64)
                            sp.wait_ge(x_stored[0], 32)
                            sp.wait_ge(x_stored[1], 32)
                            sp.wait_ge(pair_free[j], i + Q_OUT // 2)
                            sp.dma_start(x_res[:, j, :, :], x_fm[:, ds(i * 4 + 2 * j, 2), :]).then_inc(res_landed[j], 16)

            def up(base, per, i, b):
                for g in range(4):
                    col = (g % 2) * D_FF + (g // 2) * UN
                    for k in range(4):
                        src = ffi_t[:, UC * k:UC * k + UC, ds(b * (2 * UN) + col, UN)]
                        unit(base, per, i, 4 * g + k, src)

            up(G_FF0, 16, 0, 0)
            with sp.Fori(0, NBLK - 1) as i:
                up(G_FF, 24, i, i + 1)
                for j in range(8):
                    unit(G_FF, 24, i, 16 + j, ffo_t[:, ds(i * UC, UC), UN * j:UN * j + UN])
            for j in range(8):
                unit(G_FIN, 8, 0, j, ffo_t[:, UC * (NBLK - 1):UC * NBLK, UN * j:UN * j + UN])
            for t in range(4):
                sp.wait_ge(rows_scaled[t % 2], t // 2 + 1)
                sp.dma_start(out[0, P * t:P * t + P, :], out_tm[:, t, :]).then_inc(out_stored, 16)
            sp.wait_ge(out_stored, 64)

        @block.scalar
        def _(act):
            chain = Chain(act, act_chain)

            def hi(base, per, i, u):
                landed(act, base, per, i, u)
                act.activation(w_hi[:, u % RING], w_raw[:, u % RING], ACT.Copy).then_inc(hi_done, 1)

            rows = [(0, 0, b_ada[0], 96), (0, 96, norm1_g[0], 16), (0, 112, norm2_g[0], 16),
                    (1, 0, b_gate[0], 48), (1, 48, pool_scale[0], 16), (1, 64, conv_w[0], 32),
                    (1, 96, conv_b[0], 8), (1, 104, norm_f_g, 16),
                    (2, 0, lru_ba[0], 16), (2, 16, lru_bx[0], 16), (2, 32, lru_lambda[0], 16),
                    (2, 48, c, 16), (2, 64, c_ctx, 16)]
            for r, first, src, n in rows:
                if len(src.shape) == 1:
                    src = src.rearrange("(a b) -> a b", b=P)
                elif len(src.shape) == 3:
                    src = src.rearrange("d h b -> (d h) b")
                else:
                    src = src.rearrange("d (a b) -> (d a) b", b=P)
                act.dma_start(prm_rows[first:first + n, r, :], src).then_inc(prm_landed[r], 16)
            act.wait_ge(prm_ready, 1)
            act.activation(cvec[:, :, 0], prm[:, C_C:C_C + 16], ACT.Silu)
            act.activation(cvec[:, :, 1], prm[:, C_CC:C_CC + 16], ACT.Silu).then_inc(cvec_ready, 1)
            act.wait_ge(nabs_ready, 1)
            act.activation(lam[:, 2, :], lam[:, 1, :], ACT.Exp).then_inc(z_ready, 1)
            for i in range(6):
                act.wait_ge(tok_landed[i % 2], 16 * (i // 2 + 1))
                if i >= 2:
                    act.wait_ge(nrm_turned, 4 * (i - 1))
                chain.link(act.activation(x_nrm[:, i % 2, :], x_tok[:, i % 2, :], ACT.Square, accum_out=ssum[:, i:i + 1]))
                act.activation(rstd[:, i:i + 1], ssum[:, i:i + 1], ACT.Sqrt, bias=eps_t[:, :], scale=1.0 / D).then_inc(root_done, 1)
                if i < 4:
                    if i >= 2:
                        act.wait_ge(x_stored[i % 2], 16)
                    for q in range(4):
                        act.wait_ge(raw_turned, 4 * i + q + 1)
                        act.activation(x_stage[:, i % 2, 4 * q:4 * q + 4, :],
                                       main[:, q % 2, :].rearrange("p (a b) -> p a b", b=P), ACT.Copy).then_inc(raw_out, 1)
            for u in range(2):
                hi(0, 8, 0, u)
            for s in range(2):
                act.wait_ge(x_stored[s], 32)
            with act.Fori(0, 4) as q:
                for k in range(2):
                    act.wait_ge(ada_used, q * 8 + 4 * k + 4)
                    act.wait_ge(row_turned, q * 2)
                    act.activation(ada_row[0:2, k, :], aux[0:2, k, :], ACT.Copy).then_inc(row_out, 1)
                for t in range(4):
                    act.wait_ge(u_aff, q * 8 + 2 * t + 1)
                    act.activation(u_hi[:, ds(q * 4 + t, 1), :], u_f[:, ds(q * 4 + t, 1), :], ACT.Copy).then_inc(u_hi_done, 1)
                    act.wait_ge(u_aff, q * 8 + 2 * t + 2)
                    act.activation(ctx_hi[:, ds(q * 4 + t, 1), :], ctx_f[:, ds(q * 4 + t, 1), :], ACT.Copy).then_inc(u_hi_done, 1)

            with act.Fori(0, 2) as i:
                for u in range(8):
                    hi(G_XA, 8, i, u + 2)
                    if u % 4 == 3:
                        j = u // 4
                        if u == 3:
                            act.wait_ge(ada_used, 32)
                        act.wait_ge(unit_used, i * 8 + u + 1)
                        act.activation(pad[:, ds(i * 4 + 2 * j, 2), PADX:PADX + T], main[:, 2 * j:2 * j + 2, :],
                                       ACT.Copy).then_inc(pair_free[j], 1)

            def decay(h, d):
                hd = d * 8 + h
                act.wait_ge(gates_done, h * 2 + d + 1)
                act.activation(la[:, d, :], aux_flat[:, 256:1024], ACT.Tanh, bias=prm_h(C_BA, d, h), scale=0.5)
                act.activation(lb[:, d, :], aux_flat[:, 1280:2048], ACT.Tanh, bias=prm_h(C_BX, d, h), scale=0.5).then_inc(tanh_done, 1)
                act.wait_ge(tanh_done, h * 2 + d + 1)
                cc = c2[:, ds(hd, 1)]
                act.activation(lt[:, d, :], la[:, d, :], ACT.Tanh, bias=cc, scale=cc)
                act.activation(la[:, d, :], la[:, d, :], ACT.Exp, bias=cc, scale=cc).then_inc(decay_done, 1)

            def prm_h(col, d, h):
                return prm[:, ds(h + (col + 8 * d), 1)]

            def roots(h):
                for d in range(2):
                    act.wait_ge(q_done, h * 2 + d + 1)
                    act.activation(lt[:, d, :], lt[:, d, :], ACT.Sqrt, scale=-0.25).then_inc(root_q, 1)

            def gelu(h, p, copies):
                act.wait_ge(pair_free[p], copies)
                act.activation(yx[:, ds(h, 1), :], yx[:, ds(h, 1), :], ACT.Gelu_apprx_tanh).then_inc(gelu_done, 1)

            def product_hi(h):
                act.wait_ge(prod_done, h + 1)
                act.activation(act_r[:, ds(h, 1), 0, :], act_f[:, ds(h, 1), 1, :], ACT.Copy).then_inc(act_hi, 1)

            def window(h, hh, p, base, per, i, u0, first=False):
                for u in range(4):
                    hi(base, per, i, u0 + u + 2)
                    if u == 1 and not first:
                        gelu(h - 1, 1 - p, hh + 3)
                    if u == 0 and not first:
                        roots(h - 1)
                    if u == 2:
                        if not first:
                            act.wait_ge(lru_done, h)
                        decay(h, 0)
                    if u == 3:
                        if not first:
                            product_hi(h - 1)
                        decay(h, 1)
                act.wait_ge(unit_used, base + u0 + 4 + i * per)
                act.activation(yx[:, ds(h * 2, 2), :], main[:, 2 * p:2 * p + 2, :], ACT.Copy).then_inc(pair_free[p], 1)

            act.wait_ge(c2_ready, 1)
            window(0, 0, 0, G_YX, 4, 0, 0, first=True)
            with act.Fori(0, 3) as i:
                window(i * 2 + 1, i, 1, G_YX + 4, 8, i, 0)
                window(i * 2 + 2, i, 0, G_YX + 4, 8, i, 4)
            window(7, 3, 1, G_YX + 28, 4, 0, 0)

            def chunk_out(t):
                p = (Q_FOUR + t) % 2
                if t >= 2:
                    act.wait_ge(chunk_used, t - 1)
                act.wait_ge(chunk_ready, t + 1)
                act.activation(xcs[:, t % 2, :, :], main[:, 2 * p:2 * p + 2, :].rearrange("p b (g n) -> p (b g) n", n=256),
                               ACT.Copy).then_inc(pair_free[p], 1)

            chunk_out(0)
            chunk_out(1)
            roots(7)
            gelu(7, 1, 6)
            chunk_out(2)
            chunk_out(3)
            product_hi(7)
            act.wait_ge(chunk_used, 4)
            for g in range(4):
                act.wait_ge(four_done, g + 1)
                act.activation(four_hi[:, g, :], four_f[:, g, :], ACT.Copy).then_inc(four_hi_done, 1)

            with act.Fori(0, 8) as i:
                chain.enter(i, 0, 1)

                def ada2(cc):
                    s = cc % 2
                    act.wait_ge(ada2_used[s], i * 8 + cc // 2)
                    act.dma_start(ada2_pc[:, s, :], ada_t[:, cc, ds(i * 1024 + 2 * D, 1024)]).then_inc(ada2_landed[s], 16)

                for u in range(16):
                    if u + 2 != POOL_AT:
                        hi(G_MIX, 16, i, u + 2)
                    if u == 1:
                        chain.link(act.activation(spare[:, :], eps_t[:, :], ACT.Sigmoid))
                    if u == 0:
                        ada2(0)
                    if u < 15:
                        ada2(u + 1)
                    if u in (3, 8, 13):
                        k = (3, 8, 13).index(u)
                        branch = (1, 2, 0)[k]
                        act.wait_ge(unit_used, i * 16 + (G_MIX + u + 1))
                        if k == 1:
                            act.wait_ge(pair_free[1], i * 3 + (Q_MIX // 2 + 1))
                        else:
                            act.wait_ge(gate_used, i * 2 + k // 2)
                        for n in range(2):
                            ins = act.activation(gate[:, n, :], main[:, n, :], ACT.Sigmoid,
                                                 bias=prm[:, ds(i * 2 + (C_BG + 16 * branch + n), 1)])
                        ins.then_inc(pair_free[0], 1)
                chain.leave(8)
            for k in range(KT):
                if k in (0, 14):
                    act.wait_ge(gate_used, 14 + k // 7)
                    act.wait_ge(unit_used, G_OUT - 2)
                act.activation(u_hi[:, k, :], mixed[:, k, :], ACT.Copy).then_inc(m_hi, 1)

            with act.Fori(0, 4) as i:
                for u in range(8):
                    hi(G_OUT, 8, i, u + 2)
                    if u % 4 == 3:
                        j = u // 4
                        act.wait_ge(pair_free[j], i + (Q_OUT // 2 + 1))
                        act.wait_ge(sq_added, i * 2 + j + 1)
                        act.activation(sq[:, :, :], mixed[:, ds(i * 4 + 2 * j, 2), :], ACT.Square).then_inc(sq_done, 1)
            hi(G_FF0, 16, 0, 2)
            hi(G_FF0, 16, 0, 3)
            chain.link(act.activation(spare[:, :], eps_t[:, :], ACT.Sqrt))
            act.wait_ge(ms_ready, 1)
            act.activation(rstd_b[:, :], aux[:, 0, :], ACT.Sqrt, bias=eps_t[:, :], scale=1.0 / D).then_inc(rms_ready, 1)
            for k in range(KT):
                act.wait_ge(v_aff, k + 1)
                act.activation(u_hi[:, k, :], u_f[:, k, :], ACT.Identity, bias=mod2[:, 16 + k:17 + k]).then_inc(v_hi, 1)

            def up_steps(base, per, i, b, q0, qi):
                pos = ds(b % 2, 1) if not isinstance(b, int) else slice(b % 2, b % 2 + 1)
                for u in range(16):
                    if base != G_FF0 or u >= 2:
                        hi(base, per, i, u + 2)
                    pr = u // 8
                    if u % 8 == 3:
                        act.wait_ge(unit_used, base + u + 1 + i * per)
                        act.wait_ge(pair_free[1], q0 // 2 + pr + i * qi)
                        act.activation(gate[:, :, :], main[:, 0:2, :], ACT.Silu).then_inc(pair_free[0], 1)
                    if u % 8 == 7:
                        act.wait_ge(pair_free[1], q0 // 2 + pr + 1 + i * qi)
                        f = ff_f[:, pos, 1, 2 * pr:2 * pr + 2, :].rearrange("p o a n -> p (o a) n")
                        h = ff_r[:, pos, 0, 2 * pr:2 * pr + 2, :].rearrange("p o a n -> p (o a) n")
                        act.activation(h, f, ACT.Copy).then_inc(hid_hi, 1)

            up_steps(G_FF0, 16, 0, 0, Q_FF0, 2)
            with act.Fori(0, NBLK - 1) as i:
                up_steps(G_FF, 24, i, i + 1, Q_FF, 6)
                for u in range(16, 24):
                    hi(G_FF, 24, i, u + 2)

            def fin_evac(p):
                b = 2 * (p % 2) + 1
                act.wait_ge(fin_turned, p + 1)
                act.activation(out_tm[:, :, (2 * p + 1) * P:(2 * p + 2) * P],
                               aux[:, b, :].rearrange("p (t f) -> p t f", f=P), ACT.Copy).then_inc(fin_out_a, 1)

            for p in range(8):
                if p + 2 < 8:
                    hi(G_FIN, 8, 0, p + 2)
                act.wait_ge(pair_free[p % 2], Q_FIN // 2 + p // 2 + 1)
                if p:
                    act.wait_ge(sq2_added, p)
                act.activation(sq[:, :, :], mixed[:, 2 * p:2 * p + 2, :], ACT.Square).then_inc(sq2_done, 1)
                if p >= 2:
                    act.wait_ge(fin_turned, p - 1)
                for n in range(2):
                    ins = act.activation(x_fin[:, p % 2, n, :], mixed[:, 2 * p + n, :], ACT.Copy,
                                         scale=prm[:, C_NF + 2 * p + n:C_NF + 2 * p + n + 1])
                ins.then_inc(fin_ready, 1)
                if p:
                    fin_evac(p - 1)
            fin_evac(7)
            act.wait_ge(ms2_ready, 1)
            act.activation(rfin[:, :], main[:, 0, 0:4], ACT.Sqrt, bias=eps_t[:, :], scale=1.0 / D).then_inc(rms2_ready, 1)
            act.wait_ge(rfin_ready, 1)
            act.wait_ge(fin_out_v, 8)
            act.wait_ge(fin_out_a, 8)
            for t in (1, 3):
                act.activation(out_tm[:, t, :], out_tm[:, t, :], ACT.Copy, scale=rfin[:, t:t + 1]).then_inc(rows_scaled[1], 1)

        @block.tensor
        def _(pe):
            def triple(dst, slot, cc, n, m_hi_ap, m_lo_ap, start, stop):
                wh = w_hi[:, slot, cc, n * P:n * P + P]
                wl = w_lo[:, slot, cc, n * P:n * P + P]
                pe.matmul(dst, wh, m_hi_ap, start=start, stop=False)
                pe.matmul(dst, wh, m_lo_ap, start=False, stop=False)
                return pe.matmul(dst, wl, m_hi_ap, start=False, stop=stop)

            def unit(base, per, i, u, p, moving, first, last, ready=None):
                pe.wait_ge(lo_done, splits(base, per, i, u))
                for n in range(2):
                    for cc in range(UC):
                        if ready and n == 0:
                            pe.wait_ge(ready[0], ready[1] + cc)
                        h, l = moving(cc)
                        ins = triple(main[:, 2 * p + n, :], u % RING, cc, n, h, l,
                                     first and cc == 0, last and cc == UC - 1)
                ins.then_inc(unit_used, 1)

            def u_of(k):
                return lambda cc: (u_hi[:, UC * k + cc, :], u_lo[:, UC * k + cc, :])

            pe.wait_ge(const_landed, 16)
            col = 0
            for r, n in enumerate(PRM_ROWS):
                pe.wait_ge(prm_landed[r], 16 * (3, 5, 5)[r])
                ins = pe.transpose(main[:, 0, col:col + n], prm_rows[0:n, r, :], ident[0:n, 0:n])
                col += n
            ins.then_inc(prm_turned, 1)
            pe.wait_ge(prm_ready, 1)

            def turn_tile(i):
                if i < 4:
                    pe.wait_ge(tok_landed[i % 2], 16 * (i // 2 + 1))
                    for q in range(4):
                        if 4 * i + q >= 2:
                            pe.wait_ge(raw_out, 4 * i + q - 1)
                        for a in range(4):
                            ins = pe.transpose(main[:, q % 2, a * P:a * P + P], x_tok[:, i % 2, (4 * q + a) * P:(4 * q + a + 1) * P], ident)
                        ins.then_inc(raw_turned, 1)
                pe.wait_ge(nrm_done, i + 1)
                for q in range(4):
                    if 4 * i + q >= 2:
                        pe.wait_ge(nrm_out, 4 * i + q - 1)
                    for a in range(4):
                        ins = pe.transpose(main[:, 2 + q % 2, a * P:a * P + P], x_nrm[:, i % 2, (4 * q + a) * P:(4 * q + a + 1) * P], ident)
                    ins.then_inc(nrm_turned, 1)

            def ada_piece(q, k, j):
                pe.wait_ge(ada_landed[j], q * 32 + 16 * k + 16)
                for cc in range(4):
                    ins = pe.matmul(aux[0:2, k, :], cvec[:, 4 * j + cc, :], ada_pc[:, j, cc, :],
                                    start=(j == 0 and cc == 0), stop=(j == 3 and cc == 3))
                ins.then_inc(ada_used, 1)

            def turn_row(k):
                for t in range(4):
                    ins = pe.transpose(aux[:, 2 + k, 2 * t:2 * t + 2], ada_row[0:2, k, t * P:t * P + P], ident[0:2, 0:2])
                ins.then_inc(row_turned, 1)

            for i in range(6):
                turn_tile(i)
                if i == 0:
                    pe.wait_ge(cvec_ready, 1)
                for j in ((0,), (1,), (2,), (3,), (4, 5), (6, 7))[i]:
                    ada_piece(0, j // 4, j % 4)
                    if j == 6:
                        pe.wait_ge(row_out, 1)
                        turn_row(0)
            with pe.Fori(1, 4) as q:
                for k in range(2):
                    pe.wait_ge(row_out, q * 2 + (k - 1))
                    for j in range(4):
                        if j == 1:
                            pe.wait_ge(row_out, q * 2 + k)
                            pe.wait_ge(mod_out, q * 2 + (k - 2))
                        ada_piece(q, k, j)
                        if j == 1:
                            turn_row(1 - k)
            pe.wait_ge(row_out, 8)
            turn_row(1)

            with pe.Fori(0, 2) as i:
                for j in range(2):
                    pe.wait_ge(pair_free[j], i)
                    pe.wait_ge(ctx_free[j], i)
                    for k in range(4):
                        u = 4 * j + k
                        pe.wait_ge(u_lo_done, 8 * k + 8)
                        pe.wait_ge(lo_done, splits(G_XA, 8, i, u))
                        for n in range(2):
                            for cc in range(UC):
                                kt = UC * k + cc
                                s, e = kt == 0, kt == KT - 1
                                triple(main[:, 2 * j + n, :], u % RING, cc, n, u_hi[:, kt, :], u_lo[:, kt, :], s, e)
                                ins = triple(aux[:, 2 * j + n, 0:TC], u % RING, cc, n, ctx_hi[:, kt, :], ctx_lo[:, kt, :], s, e)
                        ins.then_inc(unit_used, 1)

            def gates(h, hh, p, d):
                pe.wait_ge(gw_landed[p], hh * 32 + 32)
                pe.wait_ge(conv_done, h + 1)
                if not isinstance(h, int) or h or d:
                    pe.wait_ge(tanh_done, h * 2 + d)
                for ty in range(2):
                    w = gate_w[:, p, ty, d, :]
                    pe.matmul(aux[:, 2 * ty, TC:2 * TC], w, xcv[:, 0:TC], start=True, stop=True)
                    ins = pe.matmul(aux[:, 2 * ty + 1, :], w, xcv[:, TC:TCAT], start=True, stop=True)
                ins.then_inc(gates_done, 1)

            def window(h, hh, p, base, per, i, u0):
                pe.wait_ge(pair_free[p], hh + 2)
                for k in range(4):
                    unit(base, per, i, u0 + k, p, u_of(k), k == 0, k == 3)
                    if k in (1, 2):
                        gates(h, hh, p, k - 1)

            for j in range(2):
                pe.wait_ge(ctx_free[j], 2)
            window(0, 0, 0, G_YX, 4, 0, 0)
            with pe.Fori(0, 3) as i:
                window(i * 2 + 1, i, 1, G_YX + 4, 8, i, 0)
                window(i * 2 + 2, i + 1, 0, G_YX + 4, 8, i, 4)
            window(7, 3, 1, G_YX + 28, 4, 0, 0)

            def channels(t):
                p = (Q_FOUR + t) % 2
                pe.wait_ge(pair_free[p], (Q_FOUR + t) // 2)
                for g in range(4):
                    ins = pe.matmul(main[:, 2 * p + g // 2, (g % 2) * 256:(g % 2) * 256 + 256],
                                    yx[:, 12 + g, t * P:t * P + P], cs128, start=True, stop=True)
                ins.then_inc(chunk_ready, 1)

            def tokens(t):
                p = (Q_FOUR + t) % 2
                pe.wait_ge(dft_landed[t], 16)
                pe.wait_ge(pair_free[p], (Q_FOUR + t) // 2 + 1)
                for g in range(4):
                    pe.matmul(aux[:, g, 0:NCOS], xcs[:, t % 2, g, 0:P], dft_t[:, t, 0:NCOS], start=(t == 0), stop=False)
                    ins = pe.matmul(aux[:, g, NCOS:T], xcs[:, t % 2, g, P:2 * P], dft_t[:, t, NCOS:T], start=False, stop=(t == 3))
                ins.then_inc(chunk_used, 1)

            pe.wait_ge(pair_free[0], 6)
            pe.wait_ge(pair_free[1], 6)
            pe.wait_ge(tanh_done, 16)
            channels(0)
            channels(1)
            tokens(0)
            channels(2)
            tokens(1)
            channels(3)
            tokens(2)
            tokens(3)

            with pe.Fori(0, 8) as i:
                u = 0
                for j, what in enumerate(("g", "pool", "g", "four", "g", "lru")):
                    p = j % 2
                    pe.wait_ge(pair_free[p], i * 3 + (Q_MIX // 2 + j // 2))
                    if what == "g":
                        for k in range(4):
                            unit(G_MIX, 16, i, u, p, u_of(k), k == 0, k == 3)
                            u += 1
                    elif what == "pool":
                        landed(pe, G_MIX, 16, i, u)
                        pe.wait_ge(pool_done, 4)
                        for n in range(2):
                            ins = pe.matmul(main[:, 2 * p + n, :], w_raw[:, u % RING, 0, n * P:n * P + P],
                                            yx[:, ds(i // 2 + 8, 1), :].rearrange("p o n -> p (o n)"), start=True, stop=True)
                        ins.then_inc(unit_used, 1)
                        u += 1
                    elif what == "four":
                        pe.wait_ge(four_lo_done, 4)
                        unit(G_MIX, 16, i, u, p, lambda cc: (four_hi[:, cc, :], four_lo[:, cc, :]), True, True)
                        u += 1
                    else:
                        pe.wait_ge(act_lo, 8)
                        for k in range(2):
                            unit(G_MIX, 16, i, u, p, lambda cc: (act_r[:, UC * k + cc, 0, :], act_r[:, UC * k + cc, 1, :]), k == 0, k == 1)
                            u += 1
                pe.wait_ge(ada2_used[1], i * 8 + 8)
                for t in range(8):
                    ins = pe.matmul(aux[:, 0, ds(i * 8 + t, 1)], ada2_acc[:, t * P:t * P + P], ones[:, 0:1], start=True, stop=True)
                ins.then_inc(acc_used, 1)

            with pe.Fori(0, 4) as i:
                for j in range(2):
                    pe.wait_ge(pair_free[j], i + Q_OUT // 2)
                    for k in range(4):
                        pe.wait_ge(m_lo, UC * k + UC)
                        unit(G_OUT, 8, i, 4 * j + k, j, u_of(k), k == 0, k == 3)
            pe.wait_ge(sq_added, 8)
            for n in range(2):
                pe.matmul(aux[:, 0, :], ones[:, :], sq_acc[:, n, :], start=(n == 0), stop=False)
            pe.wait_ge(sq_done, 8)
            for n in range(2):
                ins = pe.matmul(aux[:, 0, :], ones[:, :], sq[:, n, :], start=False, stop=(n == 1))
            ins.then_inc(ms_ready, 1)

            def up(base, per, i, q0, qi):
                for g in range(4):
                    p = g % 2
                    pe.wait_ge(pair_free[p], q0 // 2 + g // 2 + i * qi)
                    for k in range(4):
                        ready = (v_lo, UC * k + 1) if base == G_FF0 and g == 0 else None
                        unit(base, per, i, 4 * g + k, p, u_of(k), k == 0, k == 3, ready)

            def hid(buf):
                if isinstance(buf, int):
                    return lambda cc: (ff_r[:, buf, 0, cc, :], ff_r[:, buf, 1, cc, :])
                return lambda cc: tuple(ff_r[:, ds(buf, 1), s, cc, :].rearrange("p o n -> p (o n)") for s in range(2))

            up(G_FF0, 16, 0, Q_FF0, 2)
            with pe.Fori(0, NBLK - 1) as i:
                up(G_FF, 24, i, Q_FF, 6)
                pe.wait_ge(hid_lo, i * 2 + 2)
                for j in range(8):
                    pe.wait_ge(pair_free[j % 2], i * 6 + (Q_FF // 2 + 2 + j // 2))
                    unit(G_FF, 24, i, 16 + j, j % 2, hid(i % 2), True, True)

            def turn(p):
                pe.wait_ge(fin_ready, p + 1)
                if p >= 2:
                    pe.wait_ge(fin_out_a, p - 1)
                    pe.wait_ge(fin_out_v, p - 1)
                for n in range(2):
                    for t in range(4):
                        ins = pe.transpose(aux[:, 2 * (p % 2) + n, t * P:t * P + P], x_fin[:, p % 2, n, t * P:t * P + P], ident)
                ins.then_inc(fin_turned, 1)

            pe.wait_ge(hid_lo, 2 * NBLK)
            for j in range(8):
                pe.wait_ge(pair_free[j % 2], Q_FIN // 2 + j // 2)
                unit(G_FIN, 8, 0, j, j % 2, hid((NBLK - 1) % 2), True, True)
                if j:
                    turn(j - 1)
            turn(7)
            pe.wait_ge(sqf2_ready, 1)
            for t in range(4):
                ins = pe.matmul(main[:, 0, t:t + 1], sq[:, 0, t * P:t * P + P], ones[:, 0:1], start=True, stop=True)
            ins.then_inc(ms2_ready, 1)

        @block.gpsimd
        def _(pool):
            link = Chain(pool, pool_chain).link

            pool.wait_ge(const_landed, 16)
            pool.wait_ge(pair_free[0], 5)
            pool.wait_ge(pair_free[1], 5)
            pool.memset(pw_a[:, :, 0:8], 0.0)
            link(pool.memset(pw_a[:, :, 72:80], 0.0))
            for g in range(4):
                xb = yx[:, 8 + g, :].rearrange("p (r w) -> p r w", w=GRID_W)
                if g:
                    pool.wait_ge(pool_done, g)
                    pool.memset(pw_a[:, :, 0:8], 0.0)
                    pool.memset(pw_a[:, :, 72:80], 0.0)
                link(pool.tensor_copy(pw_a[:, :, 8:72], xb))
                src, dst, n = pw_a, pw_b, 80
                for k in range(g + 1):
                    n -= 1 << k
                    link(pool.tensor_tensor(dst[:, :, 0:n], src[:, :, 0:n], src[:, :, (1 << k):(1 << k) + n], ALU.add))
                    src, dst = dst, src
                half = 1 << g
                mean = dst[:, :, 0:GRID_W]
                cnt = inv_cnt[:, GRID_W * g:GRID_W * (g + 1)].unsqueeze(1).to_broadcast([P, ROWS, GRID_W])
                link(pool.tensor_tensor(mean, src[:, :, 8 - half:8 - half + GRID_W], cnt, ALU.mult))
                pool.tensor_tensor(xb, mean, xb, ALU.subtract).then_inc(pool_done, 1)

        @block.vector
        def _(dve):
            chain = Chain(dve, dve_chain)
            link = chain.link

            def lo(base, per, i, u):
                s = u % RING
                dve.wait_ge(hi_done, splits(base, per, i, u))
                dve.tensor_tensor(w_lo[:, s], w_raw[:, s], w_hi[:, s].bitcast(F32), ALU.subtract).then_inc(lo_done, 1)

            dve.memset(ones[:, :], 1.0)
            link(dve.memset(eps_t[:, :], EPS))
            dve.wait_ge(prm_turned, 1)
            dve.tensor_copy(prm[:, :], main[:, 0, 0:NPRM]).then_inc(prm_ready, 1)
            dve.wait_ge(prm_ready, 1)
            for col in (C_BA, C_BX):
                link(dve.tensor_scalar(prm[:, col:col + 16], prm[:, col:col + 16], 0.5, None, ALU.mult))
            lam_p = prm[:, C_LAM:C_LAM + 16]
            link(dve.tensor_scalar(lam[:, 0, :], lam_p, -1.0, None, ALU.mult))
            dve.tensor_tensor(lam[:, 1, :], lam[:, 0, :], lam_p, ALU.min).then_inc(nabs_ready, 1)
            for i in range(6):
                dve.wait_ge(root_done, i + 1)
                dve.wait_ge(tok_landed[i % 2], 16 * (i // 2 + 1))
                link(dve.reciprocal(rstd[:, i:i + 1], rstd[:, i:i + 1]))
                dve.tensor_scalar(x_nrm[:, i % 2, :], x_tok[:, i % 2, :], rstd[:, i:i + 1], None, ALU.mult).then_inc(nrm_done, 1)
                for q in range(4):
                    dve.wait_ge(nrm_turned, 4 * i + q + 1)
                    dst = u_f[:, 4 * q:4 * q + 4, P * i:P * i + P] if i < 4 else ctx_f[:, 4 * q:4 * q + 4, P * (i - 4):P * (i - 3)]
                    dve.tensor_copy(dst, main[:, 2 + q % 2, :].rearrange("p (a b) -> p a b", b=P)).then_inc(nrm_out, 1)
            dve.wait_ge(z_ready, 1)
            z, den, s1, s2, poly = lam[:, 2, :], lam[:, 3, :], lam[:, 3, :], lam[:, 4, :], lam[:, 5, :]
            link(dve.tensor_scalar(den, z, 2.0, None, ALU.add))
            link(dve.reciprocal(den, den))
            link(dve.tensor_tensor(s1, den, z, ALU.mult))
            link(dve.tensor_tensor(s2, s1, s1, ALU.mult))
            link(dve.tensor_scalar(poly, s2, 1.0 / 15, None, ALU.mult))
            for k in (13, 11, 9, 7, 5, 3):
                link(dve.scalar_tensor_tensor(poly, poly, 1.0 / k, s2, ALU.add, ALU.mult))
            link(dve.scalar_tensor_tensor(poly, poly, 1.0, s1, ALU.add, ALU.mult))
            link(dve.tensor_scalar(lam[:, 0, :], lam[:, 0, :], 0.0, None, ALU.max))
            link(dve.scalar_tensor_tensor(poly, poly, 2.0, lam[:, 0, :], ALU.mult, ALU.add))
            dve.tensor_scalar(c2[:, :], poly, 1e-20, -RGLRU_C / 2, ALU.max, ALU.mult).then_inc(c2_ready, 1)
            for u in range(2):
                lo(0, 8, 0, u)
            with dve.Fori(0, 4) as q:
                chain.enter(q, 0, 1)
                for k in range(2):
                    dve.wait_ge(row_turned, q * 2 + k + 1)
                    turned = aux[:, 2 + k, 0:8].rearrange("p (t v) -> p t v", v=2)
                    for v in range(2):
                        ins = dve.tensor_tensor(mod1[:, v, k, ds(q * 4, 4)], turned[:, :, v],
                                                prm[:, ds(q * 4 + (C_BADA + 16 * k), 4)], ALU.add)
                    ins.then_inc(mod_out, 1)
                dve.wait_ge(mod_out, q * 2 + 2)
                dve.scalar_tensor_tensor(gsc1[:, 0, ds(q * 4, 4)], mod1[:, 0, 1, ds(q * 4, 4)], 1.0,
                                         prm[:, ds(q * 4 + C_N1, 4)], ALU.add, ALU.mult)
                link(dve.scalar_tensor_tensor(gsc1[:, 1, ds(q * 4, 4)], mod1[:, 1, 1, ds(q * 4, 4)], 1.0,
                                              prm[:, ds(q * 4 + C_N1, 4)], ALU.add, ALU.mult))
                for t in range(4):
                    k = ds(q * 4 + t, 1)
                    for v, f in enumerate((u_f, ctx_f)):
                        dve.tensor_scalar(f[:, k, :], f[:, k, :], gsc1[:, v, k], mod1[:, v, 0, k],
                                          ALU.mult, ALU.add).then_inc(u_aff, 1)
                for t in range(4):
                    k = ds(q * 4 + t, 1)
                    for v, (f, l, h) in enumerate(((u_f, u_lo, u_hi), (ctx_f, ctx_lo, ctx_hi))):
                        dve.wait_ge(u_hi_done, q * 8 + 2 * t + v + 1)
                        dve.tensor_tensor(l[:, k, :], f[:, k, :], h[:, k, :].bitcast(F32), ALU.subtract).then_inc(u_lo_done, 1)
                chain.leave(4)

            dve.wait_ge(ada_used, 32)
            dve.memset(pad[:, :, 0:2], 0.0)
            dve.memset(pad[:, :, 2 + TC:PADX], 0.0)
            link(dve.memset(pad[:, :, PADX + T:PADX + T + 1], 0.0))
            with dve.Fori(0, 2) as i:
                for u in range(8):
                    lo(G_XA, 8, i, u + 2)
                    if u % 4 == 3:
                        j = u // 4
                        dve.wait_ge(unit_used, i * 8 + u + 1)
                        dve.tensor_copy(pad[:, ds(i * 4 + 2 * j, 2), 2:2 + TC], aux[:, 2 * j:2 * j + 2, 0:TC]).then_inc(ctx_free[j], 1)

            def conv(h):
                row = ds(h, 1)

                def tap(k):
                    return prm[:, ds(h + (C_CW + 8 * k), 1)]

                if not isinstance(h, int) or h:
                    dve.wait_ge(gated, h * 2)
                for k in range(4):
                    for a, b, n in ((0, 0, TC), (TC, PADX - 2, T)):
                        src = pad[:, row, b + k:b + k + n].rearrange("p o n -> p (o n)")
                        dst = xcv[:, a:a + n]
                        if k == 0:
                            ins = dve.tensor_scalar(dst, src, tap(0), prm[:, ds(h + C_CB, 1)], ALU.mult, ALU.add)
                        else:
                            ins = dve.scalar_tensor_tensor(dst, src, tap(k), dst, ALU.mult, ALU.add)
                    if k < 3:
                        link(ins)
                ins.then_inc(conv_done, 1)

            def mid(h):
                for d in range(2):
                    dve.wait_ge(decay_done, h * 2 + d + 1)
                    dve.wait_ge(q_done, h * 2 + d)
                    link(dve.tensor_tensor(ld[:, :], la[:, d, :], la[:, d, :], ALU.mult))
                    dve.scalar_tensor_tensor(lt[:, d, :], ld[:, :], 1.0, lt[:, d, :], ALU.add, ALU.mult).then_inc(q_done, 1)

            def gate_input(h):
                for d in range(2):
                    dve.wait_ge(tanh_done, h * 2 + d + 1)
                    dve.scalar_tensor_tensor(lb[:, d, :], lb[:, d, :], 1.0, xcv[:, :], ALU.add, ALU.mult).then_inc(gated, 1)

            def final(h):
                for d in range(2):
                    dve.wait_ge(root_q, h * 2 + d + 1)
                    dve.wait_ge(gated, h * 2 + d + 1)
                    link(dve.tensor_tensor(lb[:, d, :], lb[:, d, :], lt[:, d, :], ALU.mult))
                    a_c, b_c, s_c = la[:, d, 0:TC], lb[:, d, 0:TC], lcs[:, :]
                    a_x, b_x, s_x = la[:, d, TC:TCAT], lb[:, d, TC:TCAT], lh[:, d, :]
                    end = lcs[:, TC - 1:TC]
                    if d:
                        a_c, b_c, s_c, a_x, b_x, s_x = (v[:, ::-1] for v in (a_c, b_c, s_c, a_x, b_x, s_x))
                        end = lcs[:, 0:1]
                    link(dve.tensor_tensor_scan(s_c, a_c, b_c, 0.0, ALU.mult, ALU.add))
                    link(dve.tensor_tensor_scan(s_x, a_x, b_x, end, ALU.mult, ALU.add))
                dve.tensor_tensor(pad[:, ds(h, 1), 0:T].rearrange("p o n -> p (o n)"), lh[:, 0, :], lh[:, 1, :], ALU.add).then_inc(lru_done, 1)

            def product(h):
                dve.wait_ge(lru_done, h + 1)
                dve.wait_ge(gelu_done, h + 1)
                dve.tensor_tensor(act_f[:, ds(h, 1), 1, :], pad[:, ds(h, 1), 0:T], yx[:, ds(h, 1), :], ALU.mult).then_inc(prod_done, 1)

            def product_lo(h):
                dve.wait_ge(act_hi, h + 1)
                dve.tensor_tensor(act_r[:, ds(h, 1), 1, :], act_f[:, ds(h, 1), 1, :], act_r[:, ds(h, 1), 0, :].bitcast(F32), ALU.subtract).then_inc(act_lo, 1)

            def window(h, base, per, i, u0, first=False, last=False):
                for u in range(4):
                    lo(base, per, i, u0 + u + 2)
                    if u == 0 and not first:
                        mid(h - 1)
                        final(h - 1)
                    if u == 2 and not first:
                        product(h - 1)
                    if u == 3:
                        gate_input(h)
                        if not last:
                            conv(h + 1)
                        if not first:
                            product_lo(h - 1)

            for j in range(2):
                dve.wait_ge(pair_free[j], 2)
                dve.wait_ge(ctx_free[j], 2)
            conv(0)
            window(0, G_YX, 4, 0, 0, first=True)
            with dve.Fori(0, 3) as i:
                chain.enter(i, 0, 22)
                window(i * 2 + 1, G_YX + 4, 8, i, 0)
                window(i * 2 + 2, G_YX + 4, 8, i, 4)
                chain.leave(3)
            window(7, G_YX + 28, 4, 0, 0, last=True)
            mid(7)
            final(7)
            product(7)
            product_lo(7)

            dve.wait_ge(chunk_used, 4)
            for g in range(4):
                cos, sin = aux[:, g, 1:NCOS - 1], aux[:, g, NCOS:T]
                dve.tensor_copy(four_f[:, g, 0:NCOS:NCOS - 1], aux[:, g, 0:NCOS:NCOS - 1])
                dve.tensor_copy(four_f[:, g, 1:NCOS - 1], sin)
                link(dve.tensor_copy(four_f[:, g, NCOS:T], sin[:, ::-1]))
                dve.tensor_tensor(four_f[:, g, 1:NCOS - 1], cos, four_f[:, g, 1:NCOS - 1], ALU.add)
                dve.tensor_tensor(four_f[:, g, NCOS:T], cos[:, ::-1], four_f[:, g, NCOS:T], ALU.subtract).then_inc(four_done, 1)
            for g in range(4):
                dve.wait_ge(four_hi_done, g + 1)
                dve.tensor_tensor(four_lo[:, g, :], four_f[:, g, :], four_hi[:, g, :].bitcast(F32), ALU.subtract).then_inc(four_lo_done, 1)

            with dve.Fori(0, 8) as i:
                dst = mixed[:, ds(i * 2, 2), :]
                for u in range(16):
                    if u + 2 != POOL_AT:
                        lo(G_MIX, 16, i, u + 2)
                    s = u % 2
                    dve.wait_ge(ada2_landed[s], i * 128 + 16 * (u // 2 + 1))
                    if u == 0:
                        dve.wait_ge(pool_done, 4)
                        dve.wait_ge(acc_used, i)
                        ins = dve.tensor_scalar(ada2_acc[:, :], ada2_pc[:, s, :], cvec[:, u, 0:1], None, ALU.mult)
                    else:
                        dve.wait_ge(ada2_used[1 - s], i * 8 + (u + 1) // 2)
                        ins = dve.scalar_tensor_tensor(ada2_acc[:, :], ada2_pc[:, s, :], cvec[:, u, 0:1],
                                                       ada2_acc[:, :], ALU.mult, ALU.add)
                    ins.then_inc(ada2_used[s], 1)
                    if u in (4, 9, 15):
                        k = (4, 9, 15).index(u)
                        dve.wait_ge(unit_used, i * 16 + (G_MIX + u + 1))
                        dve.wait_ge(pair_free[0], i * 3 + (Q_MIX // 2 + k + 1))
                        if k == 0:
                            for n in range(2):
                                ins = dve.scalar_tensor_tensor(mixed[:, ds(i * 2 + n, 1), :].rearrange("p o n -> p (o n)"),
                                                               main[:, 2 + n, :], prm[:, ds(i * 2 + (C_PS + n), 1)],
                                                               gate[:, n, :], ALU.mult, ALU.mult)
                            ins.then_inc(pair_free[1], 1)
                        else:
                            dve.tensor_tensor(gate[:, :, :], main[:, 2:4, :], gate[:, :, :], ALU.mult).then_inc(pair_free[1], 1)
                            dve.wait_ge(pair_free[1], i * 3 + (Q_MIX // 2 + k + 1))
                            if k == 2:
                                dve.wait_ge(gate_used, i * 2 + 1)
                            dve.tensor_tensor(dst, dst, gate[:, :, :], ALU.add).then_inc(gate_used, 1)
            dve.wait_ge(gate_used, 16)
            for k in range(KT):
                dve.wait_ge(m_hi, k + 1)
                dve.tensor_tensor(u_lo[:, k, :], mixed[:, k, :], u_hi[:, k, :].bitcast(F32), ALU.subtract).then_inc(m_lo, 1)

            dve.wait_ge(acc_used, 8)
            link(dve.tensor_tensor(mod2[:, :], aux[:, 0, 0:64], prm[:, C_BADA + 32:C_BADA + 96], ALU.add))
            dve.scalar_tensor_tensor(gsc2[:, :], mod2[:, 32:48], 1.0, prm[:, C_N2:C_N2 + 16], ALU.add, ALU.mult)
            dve.memset(sq[:, :, :], 0.0)
            link(dve.memset(sq_acc[:, :, :], 0.0))
            with dve.Fori(0, 4) as i:
                for u in range(8):
                    lo(G_OUT, 8, i, u + 2)
                    j = u // 4
                    if u % 4 == 1:
                        dve.wait_ge(sq_done, i * 2 + j)
                        dve.wait_ge(sq_added, i * 2 + j)
                        dve.tensor_tensor(sq_acc[:, :, :], sq_acc[:, :, :], sq[:, :, :], ALU.add).then_inc(sq_added, 1)
                    if u % 4 == 3:
                        dve.wait_ge(unit_used, i * 8 + (G_OUT + u + 1))
                        dve.wait_ge(res_landed[j], i * 16 + 16)
                        for n in range(2):
                            ins = dve.scalar_tensor_tensor(mixed[:, ds(i * 4 + (2 * j + n), 1), :].rearrange("p o n -> p (o n)"),
                                                           main[:, 2 * j + n, :], mod2[:, ds(i * 4 + (2 * j + n), 1)],
                                                           x_res[:, j, n, :], ALU.mult, ALU.add)
                        ins.then_inc(pair_free[j], 1)
            lo(G_FF0, 16, 0, 2)
            lo(G_FF0, 16, 0, 3)
            dve.wait_ge(rms_ready, 1)
            link(dve.reciprocal(rstd_b[:, :], rstd_b[:, :]))
            def v_scale(k):
                dve.scalar_tensor_tensor(u_f[:, k, :], mixed[:, k, :], gsc2[:, k:k + 1], rstd_b[:, :],
                                         ALU.mult, ALU.mult).then_inc(v_aff, 1)

            v_scale(0)
            for k in range(KT):
                if k + 1 < KT:
                    v_scale(k + 1)
                dve.wait_ge(v_hi, k + 1)
                dve.scalar_tensor_tensor(u_lo[:, k, :], u_f[:, k, :], mod2[:, 16 + k:17 + k],
                                         u_hi[:, k, :].bitcast(F32), ALU.add, ALU.subtract).then_inc(v_lo, 1)

            def up_steps(base, per, i, b, q0, qi):
                for u in range(16):
                    if base != G_FF0 or u >= 2:
                        lo(base, per, i, u + 2)
                    if u % 8 == 7:
                        pr = u // 8
                        pos = ds(b % 2, 1) if not isinstance(b, int) else slice(b % 2, b % 2 + 1)
                        cols = slice(2 * pr, 2 * pr + 2)
                        f = ff_f[:, pos, 1, cols, :].rearrange("p o a n -> p (o a) n")
                        l = ff_r[:, pos, 1, cols, :].rearrange("p o a n -> p (o a) n")
                        h = ff_r[:, pos, 0, cols, :].rearrange("p o a n -> p (o a) n").bitcast(F32)
                        dve.wait_ge(unit_used, base + u + 1 + i * per)
                        dve.wait_ge(pair_free[0], q0 // 2 + pr + 1 + i * qi)
                        dve.tensor_tensor(f, gate[:, :, :], main[:, 2:4, :], ALU.mult).then_inc(pair_free[1], 1)
                        dve.wait_ge(hid_hi, b * 2 + pr + 1)
                        dve.tensor_tensor(l, f, h, ALU.subtract).then_inc(hid_lo, 1)

            def down_add(p, j):
                for n in range(2):
                    k = 2 * j + n
                    ins = dve.scalar_tensor_tensor(mixed[:, k, :], main[:, 2 * p + n, :], mod2[:, 48 + k:49 + k],
                                                   mixed[:, k, :], ALU.mult, ALU.add)
                ins.then_inc(pair_free[p], 1)

            up_steps(G_FF0, 16, 0, 0, Q_FF0, 2)
            with dve.Fori(0, NBLK - 1) as i:
                up_steps(G_FF, 24, i, i + 1, Q_FF, 6)
                for j in range(8):
                    lo(G_FF, 24, i, 16 + j + 2)
                    dve.wait_ge(unit_used, i * 24 + (G_FF + 16 + j + 1))
                    down_add(j % 2, j)

            def fin_evac(p):
                b = 2 * (p % 2)
                dve.wait_ge(fin_turned, p + 1)
                dve.tensor_copy(out_tm[:, :, 2 * p * P:(2 * p + 1) * P],
                                aux[:, b, :].rearrange("p (t f) -> p t f", f=P)).then_inc(fin_out_v, 1)

            link(dve.memset(sq_acc[:, :, :], 0.0))
            for p in range(8):
                if p + 2 < 8:
                    lo(G_FIN, 8, 0, p + 2)
                dve.wait_ge(unit_used, G_FIN + p + 1)
                down_add(p % 2, p)
                dve.wait_ge(sq2_done, p + 1)
                if p:
                    dve.wait_ge(sq2_added, p)
                dve.tensor_tensor(sq_acc[:, :, :], sq_acc[:, :, :], sq[:, :, :], ALU.add).then_inc(sq2_added, 1)
                if p:
                    fin_evac(p - 1)
            dve.wait_ge(sq2_added, 8)
            dve.tensor_tensor(sq[:, 0, :], sq_acc[:, 0, :], sq_acc[:, 1, :], ALU.add).then_inc(sqf2_ready, 1)
            fin_evac(7)
            dve.wait_ge(rms2_ready, 1)
            dve.reciprocal(rfin[:, :], rfin[:, :]).then_inc(rfin_ready, 1)
            dve.wait_ge(rfin_ready, 1)
            dve.wait_ge(fin_out_a, 8)
            dve.wait_ge(fin_out_v, 8)
            for t in (0, 2):
                dve.tensor_scalar(out_tm[:, t, :], out_tm[:, t, :], rfin[:, t:t + 1], None, ALU.mult).then_inc(rows_scaled[0], 1)


_INS = ["x", "c", "ctx", "c_ctx", "w_ada", "b_ada", "norm1_g", "norm2_g", "w_in", "conv_w", "conv_b",
        "lru_wa", "lru_ba", "lru_wx", "lru_bx", "lru_lambda", "w_lru_out", "w_pool", "pool_scale",
        "w_fourier", "b_gate", "w_out", "w_ffn_in", "w_ffn_out", "norm_f_g"]


def shape_tables():
    def wave(n):
        angle = 2 * np.pi * (np.outer(np.arange(n), np.arange(n)) % n) / n
        return np.cos(angle), np.sin(angle)

    c_ch, s_ch = wave(P)
    t = np.arange(GRID_W)
    counts = []
    for w in (2, 4, 8, 16):
        low, high = np.clip(t - w // 2, 0, GRID_W), np.clip(t - w // 2 + w, 0, GRID_W)
        counts.append(1.0 / (high - low))
    counts = np.tile(np.concatenate(counts)[None, :], (P, 1))
    consts = np.concatenate([np.eye(P), c_ch, s_ch, counts], axis=1).astype(np.float32)
    c_tok, s_tok = wave(T)
    norm = 1.0 / np.sqrt(T * P)
    dft = np.concatenate([c_tok[:, 0:NCOS] * norm, -s_tok[:, 1:NCOS - 1] * norm], axis=1).astype(np.float32)
    return consts, dft.reshape(T // P, P, T)


def kernel(**inputs):
    import concourse.bacc as bacc
    from concourse.bass_utils import run_bass_kernel_spmd

    nc = bacc.Bacc("TRN2", target_bir_lowering=False, num_devices=1, dynamic_dma_scratch_size=1024)
    arrays, args = {}, []

    def feed(name, a):
        a = np.ascontiguousarray(a)
        arrays[name] = a
        args.append(nc.dram_tensor(name, a.shape, mybir.dt.from_np(a.dtype), kind="ExternalInput").ap())

    for name in _INS:
        feed(f"in_{name}", inputs[name])
    consts, dft = shape_tables()
    feed("in_consts", consts)
    feed("in_dft", dft)
    args.append(nc.dram_tensor("out_x", (1, T, D), F32, kind="ExternalOutput").ap())
    args.append(nc.dram_tensor("x_feature_major", (P, KT, T), F32, kind="Internal").ap())
    build(nc, *args)
    result = run_bass_kernel_spmd(nc, [arrays], core_ids=[0])
    return result.results[0]["out_x"]
```
